# Optimizing a Trainium2 kernel written in Bass

```python
import math
import jax
import jax.numpy as jnp
from jax import lax
import numpy as np

D_MODEL = 1024
BATCH = 1
SEQ = 256
DEPTH = 2

RW_HEADS = 8
RW_HEAD_DIM = 64
RW_WIDTH = RW_HEADS * RW_HEAD_DIM
RW_DECAY_LORA = 64
RW_AAA_LORA = 64
RW_GATE_LORA = 128
RW_MV_LORA = 32
RW_GN_EPS = 64e-5
SSM_HEADS = 8
SSM_HEAD_DIM = 64
SSM_INNER = SSM_HEADS * SSM_HEAD_DIM
SSM_GROUPS = 2
SSM_STATE = 128
SSM_CONV = 4
SSM_CHUNK = 128
SSM_CONV_DIM = SSM_INNER + 2 * SSM_GROUPS * SSM_STATE
SSM_NORM_GROUP = SSM_INNER // SSM_GROUPS
RET_HEADS = 8
RET_HEAD_DIM = 64
RET_WIDTH = RET_HEADS * RET_HEAD_DIM
RET_CHUNK = 128
ROPE_BASE = 10000.0
N_BRANCH = 3
BRANCH_WIDTH = 512
D_FF = 2816
N_EXPERTS = 8
TOP_K = 2
D_FF_EXPERT = 3584
N_DENSE = (DEPTH + 1) // 2
N_MOE = DEPTH // 2
RMS_EPS = 1e-6

RW_COLS = 3 * RW_WIDTH + RW_DECAY_LORA + RW_AAA_LORA + RW_GATE_LORA
SSM_COLS = SSM_INNER + SSM_CONV_DIM + SSM_HEADS
RET_COLS = 4 * RET_WIDTH
GATE_COLS = N_BRANCH * D_MODEL
IN_COLS = RW_COLS + SSM_COLS + RET_COLS + GATE_COLS

kernel_name = 'hybrid_rwkv7_ssd_retention_moe'

def rms_norm(x, w):
    xf = x.astype(jnp.float32)
    y = xf * lax.rsqrt(jnp.mean(xf * xf, axis=-1, keepdims=True) + RMS_EPS)
    return (y * w.astype(jnp.float32)).astype(x.dtype)

def token_shift(x):
    return jnp.pad(x, ((0, 0), (1, 0), (0, 0)))[:, :-1]

def rwkv7_mix(p, mu, w_up, w0, a_up, a0, g_up, k_k, k_a, r_k, gn_w, gn_b, v_first, vres):
    bsz, T, _ = p.shape
    xm = p + (token_shift(p) - p) * mu
    o1, o2, o3 = RW_WIDTH, 2 * RW_WIDTH, 3 * RW_WIDTH
    o4 = o3 + RW_DECAY_LORA
    o5 = o4 + RW_AAA_LORA
    r, k, v = xm[..., :o1], xm[..., o1:o2], xm[..., o2:o3]
    xw, xa, xg = xm[..., o3:o4], xm[..., o4:o5], xm[..., o5:]
    log_decay = -jnp.exp(-jax.nn.softplus(-(w0 + jnp.tanh(xw) @ w_up)) - 0.5)
    a = jax.nn.sigmoid(a0 + xa @ a_up)
    g = jax.nn.sigmoid(xg) @ g_up
    if vres is None:
        v_first = v
    else:
        v_down, v_up, v0 = vres
        v = v + (v_first - v) * jax.nn.sigmoid(v0 + (v @ v_down) @ v_up)
    heads = lambda t: t.reshape(bsz, T, RW_HEADS, RW_HEAD_DIM)
    kk = heads(k * k_k)
    kk = kk * lax.rsqrt(jnp.maximum(jnp.sum(kk * kk, -1, keepdims=True), 1e-24))
    k = k * (1.0 + (a - 1.0) * k_a)
    r_h, k_h, v_h, a_h = heads(r), heads(k), heads(v), heads(a)
    seq_in = tuple(jnp.moveaxis(t, 1, 0) for t in
                   (r_h, heads(jnp.exp(log_decay)), k_h, v_h, -kk, kk * a_h))

    def step(state, inp):
        r_t, w_t, k_t, v_t, a_t, b_t = inp
        sa = jnp.einsum('bhij,bhj->bhi', state, a_t)
        state = (state * w_t[:, :, None, :] + sa[..., None] * b_t[:, :, None, :]
                 + v_t[..., None] * k_t[:, :, None, :])
        return state, jnp.einsum('bhij,bhj->bhi', state, r_t)

    s0 = jnp.zeros((bsz, RW_HEADS, RW_HEAD_DIM, RW_HEAD_DIM), jnp.float32)
    _, y = lax.scan(step, s0, seq_in, unroll=8)
    y = jnp.moveaxis(y, 0, 1)
    mean = jnp.mean(y, -1, keepdims=True)
    var = jnp.mean(jnp.square(y - mean), -1, keepdims=True)
    y = ((y - mean) * lax.rsqrt(var + RW_GN_EPS)).reshape(bsz, T, RW_WIDTH) * gn_w + gn_b
    bonus = jnp.sum(r_h * k_h * r_k, -1, keepdims=True) * v_h
    out = (y + bonus.reshape(bsz, T, RW_WIDTH)) * g
    return out, v_first

def causal_depthwise_conv(x, w, b):
    C = x.shape[-1]
    rhs = jnp.transpose(w).astype(x.dtype)[:, None, :]
    y = lax.conv_general_dilated(x, rhs, window_strides=(1,), padding=[(SSM_CONV - 1, 0)],
                                 dimension_numbers=('NWC', 'WIO', 'NWC'), feature_group_count=C)
    return y + b

def ssd_chunked(x, a, b, c):
    bsz, T, H, P = x.shape
    G, N = b.shape[-2], b.shape[-1]
    HG = H // G
    Q = SSM_CHUNK
    nc = T // Q
    x = x.reshape(bsz, nc, Q, G, HG, P)
    b = b.reshape(bsz, nc, Q, G, N)
    c = c.reshape(bsz, nc, Q, G, N)
    a = a.reshape(bsz, nc, Q, G, HG).transpose(0, 3, 4, 1, 2)
    a_cs = jnp.cumsum(a, axis=-1)
    causal = jnp.tril(jnp.ones((Q, Q), bool))
    seg = a_cs[..., :, None] - a_cs[..., None, :]
    L = jnp.where(causal, jnp.exp(jnp.where(causal, seg, 0.0)), 0.0)
    cb = jnp.einsum('bclgn,bcsgn->bgcls', c, b)
    y_diag = jnp.einsum('bghcls,bcsghp->bclghp', cb[:, :, None] * L, x)
    decay_states = jnp.exp(a_cs[..., -1:] - a_cs)
    states = jnp.einsum('bclgn,bghcl,bclghp->bcghpn', b, decay_states, x)
    chunk_decay = jnp.exp(a_cs[..., -1])

    def step(s, inp):
        st, dec = inp
        return dec[..., None, None] * s + st, s

    s0 = jnp.zeros((bsz, G, HG, P, N), x.dtype)
    _, prev = lax.scan(step, s0, (jnp.moveaxis(states, 1, 0), jnp.moveaxis(chunk_decay, -1, 0)))
    prev = jnp.moveaxis(prev, 0, 1)
    y_off = jnp.einsum('bclgn,bcghpn,bghcl->bclghp', c, prev, jnp.exp(a_cs))
    return (y_diag + y_off).reshape(bsz, T, H, P)

def mamba2_mix(p, conv_w, conv_b, dt_bias, a_log, d_skip, norm_w):
    bsz, T, _ = p.shape
    z = p[..., :SSM_INNER]
    xbc = p[..., SSM_INNER:SSM_INNER + SSM_CONV_DIM]
    dt = p[..., SSM_INNER + SSM_CONV_DIM:]
    xbc = jax.nn.silu(causal_depthwise_conv(xbc, conv_w, conv_b))
    nb = SSM_GROUPS * SSM_STATE
    xs = xbc[..., :SSM_INNER].reshape(bsz, T, SSM_HEADS, SSM_HEAD_DIM)
    bm = xbc[..., SSM_INNER:SSM_INNER + nb].reshape(bsz, T, SSM_GROUPS, SSM_STATE)
    cm = xbc[..., SSM_INNER + nb:].reshape(bsz, T, SSM_GROUPS, SSM_STATE)
    dt = jax.nn.softplus(dt + dt_bias)
    A = -jnp.exp(a_log)
    y = ssd_chunked(xs * dt[..., None], A * dt, bm, cm)
    y = y + d_skip[:, None] * xs
    y = y.reshape(bsz, T, SSM_INNER) * jax.nn.silu(z)
    yg = y.reshape(bsz, T, SSM_GROUPS, SSM_NORM_GROUP)
    yg = yg * lax.rsqrt(jnp.mean(yg * yg, -1, keepdims=True) + RMS_EPS)
    return yg.reshape(bsz, T, SSM_INNER) * norm_w

def rotary(t, positions):
    half = RET_HEAD_DIM // 2
    inv_freq = ROPE_BASE ** (-jnp.arange(half, dtype=jnp.float32) / half)
    ang = positions.astype(jnp.float32)[:, None] * inv_freq[None, :]
    cos = jnp.cos(ang)[None, :, None, :]
    sin = jnp.sin(ang)[None, :, None, :]
    t1, t2 = t[..., 0::2], t[..., 1::2]
    return jnp.stack([t1 * cos - t2 * sin, t1 * sin + t2 * cos], axis=-1).reshape(t.shape)

def retention_mix(p, positions):
    bsz, T, _ = p.shape
    H, Dh, Q = RET_HEADS, RET_HEAD_DIM, RET_CHUNK
    nc = T // Q
    q = rotary(p[..., :RET_WIDTH].reshape(bsz, T, H, Dh), positions)
    k = rotary(p[..., RET_WIDTH:2 * RET_WIDTH].reshape(bsz, T, H, Dh), positions) * (Dh ** -0.5)
    v = p[..., 2 * RET_WIDTH:3 * RET_WIDTH].reshape(bsz, T, H, Dh)
    g = p[..., 3 * RET_WIDTH:]
    log_gamma = jnp.log1p(-jnp.exp2(-5.0 - jnp.arange(H, dtype=jnp.float32)))
    q, k, v = (t.reshape(bsz, nc, Q, H, Dh) for t in (q, k, v))
    idx = jnp.arange(Q, dtype=jnp.float32)
    rel = idx[:, None] - idx[None, :]
    causal = rel >= 0
    decay_in = jnp.where(causal, jnp.exp(jnp.where(causal, rel, 0.0)[None] * log_gamma[:, None, None]), 0.0)
    scores = jnp.einsum('bclhd,bcshd->bchls', q, k) * decay_in
    y_in = jnp.einsum('bchls,bcshe->bclhe', scores, v)
    zeta = jnp.exp((Q - 1 - idx)[None, :] * log_gamma[:, None])
    kv = jnp.einsum('bcshd,hs,bcshe->bchde', k, zeta, v)
    chunk_decay = jnp.exp(Q * log_gamma)[:, None, None]

    def step(state, kv_c):
        return chunk_decay * state + kv_c, state

    _, prev = lax.scan(step, jnp.zeros((bsz, H, Dh, Dh), jnp.float32), jnp.moveaxis(kv, 1, 0))
    prev = jnp.moveaxis(prev, 0, 1)
    xi = jnp.exp((idx + 1.0)[None, :] * log_gamma[:, None])
    y_cross = jnp.einsum('bclhd,bchde,hl->bclhe', q, prev, xi)
    y = (y_in + y_cross).reshape(bsz, T, H, Dh)
    y = y * lax.rsqrt(jnp.mean(y * y, -1, keepdims=True) + RMS_EPS)
    return y.reshape(bsz, T, RET_WIDTH) * jax.nn.silu(g)

def swiglu(x, wg, wu, wd):
    return (jax.nn.silu(x @ wg) * (x @ wu)) @ wd

def moe_swiglu(x, router, wg, wu, wd):
    logits = (x @ router).astype(jnp.float32)
    top_v, top_i = lax.top_k(logits, TOP_K)
    top_w = jax.nn.softmax(top_v, axis=-1)
    gates = jnp.sum(jax.nn.one_hot(top_i, N_EXPERTS, dtype=jnp.float32) * top_w[..., None], axis=-2)
    gates = gates.astype(x.dtype)
    out = jnp.zeros_like(x)
    for e in range(N_EXPERTS):
        out = out + gates[..., e:e + 1] * swiglu(x, wg[e], wu[e], wd[e])
    return out

def setup_inputs(seed: int = 0) -> dict:
    key = jax.random.key(seed)
    ks = iter(jax.random.split(key, 48))
    f32 = jnp.float32

    def nrm(shape, scale):
        return jax.random.normal(next(ks), shape, f32) * scale

    def unif(shape, lo, hi):
        return jax.random.uniform(next(ks), shape, f32, lo, hi)

    L, Lv = DEPTH, DEPTH - 1
    dt_init = jnp.exp(unif((L, SSM_HEADS), math.log(1e-3), math.log(1e-1)))
    return {
        'x': nrm((BATCH, SEQ, D_MODEL), 1.0),
        'norm1_w': 1.0 + nrm((L, D_MODEL), 0.1),
        'w_in': nrm((L, D_MODEL, IN_COLS), D_MODEL ** -0.5),
        'rw_mu': unif((L, RW_COLS), 0.0, 1.0),
        'rw_w_up': nrm((L, RW_DECAY_LORA, RW_WIDTH), 0.1 * RW_DECAY_LORA ** -0.5),
        'rw_w0': unif((L, RW_WIDTH), -4.0, 1.0),
        'rw_a_up': nrm((L, RW_AAA_LORA, RW_WIDTH), 0.5 * RW_AAA_LORA ** -0.5),
        'rw_a0': nrm((L, RW_WIDTH), 0.5),
        'rw_g_up': nrm((L, RW_GATE_LORA, RW_WIDTH), RW_GATE_LORA ** -0.5),
        'rw_k_k': 0.85 + nrm((L, RW_WIDTH), 0.1),
        'rw_k_a': 1.0 + nrm((L, RW_WIDTH), 0.1),
        'rw_r_k': nrm((L, RW_HEADS, RW_HEAD_DIM), 0.1),
        'rw_gn_w': 1.0 + nrm((L, RW_WIDTH), 0.1),
        'rw_gn_b': nrm((L, RW_WIDTH), 0.01),
        'rw_v_down': nrm((Lv, RW_WIDTH, RW_MV_LORA), RW_WIDTH ** -0.5),
        'rw_v_up': nrm((Lv, RW_MV_LORA, RW_WIDTH), 0.5 * RW_MV_LORA ** -0.5),
        'rw_v0': 1.0 + nrm((Lv, RW_WIDTH), 0.1),
        'ssm_conv_w': nrm((L, SSM_CONV_DIM, SSM_CONV), SSM_CONV ** -0.5),
        'ssm_conv_b': nrm((L, SSM_CONV_DIM), 0.01),
        'ssm_dt_bias': dt_init + jnp.log(-jnp.expm1(-dt_init)),
        'ssm_a_log': jnp.log(unif((L, SSM_HEADS), 1.0, 16.0)),
        'ssm_d': 1.0 + nrm((L, SSM_HEADS), 0.1),
        'ssm_norm_w': 1.0 + nrm((L, SSM_INNER), 0.1),
        'w_branch': nrm((L, N_BRANCH, BRANCH_WIDTH, D_MODEL), BRANCH_WIDTH ** -0.5),
        'w_out': nrm((L, D_MODEL, D_MODEL), D_MODEL ** -0.5),
        'norm2_w': 1.0 + nrm((L, D_MODEL), 0.1),
        'ffn_wg': nrm((N_DENSE, D_MODEL, D_FF), D_MODEL ** -0.5),
        'ffn_wu': nrm((N_DENSE, D_MODEL, D_FF), D_MODEL ** -0.5),
        'ffn_wd': nrm((N_DENSE, D_FF, D_MODEL), D_FF ** -0.5),
        'moe_router': nrm((N_MOE, D_MODEL, N_EXPERTS), D_MODEL ** -0.5),
        'moe_wg': nrm((N_MOE, N_EXPERTS, D_MODEL, D_FF_EXPERT), D_MODEL ** -0.5),
        'moe_wu': nrm((N_MOE, N_EXPERTS, D_MODEL, D_FF_EXPERT), D_MODEL ** -0.5),
        'moe_wd': nrm((N_MOE, N_EXPERTS, D_FF_EXPERT, D_MODEL), D_FF_EXPERT ** -0.5),
        'final_norm_w': 1.0 + nrm((D_MODEL,), 0.1),
    }

def reference(x, norm1_w, w_in, rw_mu, rw_w_up, rw_w0, rw_a_up, rw_a0, rw_g_up, rw_k_k, rw_k_a,
              rw_r_k, rw_gn_w, rw_gn_b, rw_v_down, rw_v_up, rw_v0, ssm_conv_w, ssm_conv_b,
              ssm_dt_bias, ssm_a_log, ssm_d, ssm_norm_w, w_branch, w_out, norm2_w, ffn_wg,
              ffn_wu, ffn_wd, moe_router, moe_wg, moe_wu, moe_wd, final_norm_w):
    act_dtype = x.dtype
    f32 = jnp.float32
    positions = jnp.arange(x.shape[1])
    c1 = RW_COLS
    c2 = c1 + SSM_COLS
    c3 = c2 + RET_COLS
    v_first = None
    for layer in range(DEPTH):
        h = rms_norm(x, norm1_w[layer])
        wl = w_in[layer]
        p_rw = (h @ wl[:, :c1]).astype(f32)
        p_ssm = (h @ wl[:, c1:c2]).astype(f32)
        p_ret = (h @ wl[:, c2:c3]).astype(f32)
        gate_logits = h @ wl[:, c3:]
        vres = None if layer == 0 else (rw_v_down[layer - 1], rw_v_up[layer - 1], rw_v0[layer - 1])
        y_rw, v_first = rwkv7_mix(p_rw, rw_mu[layer], rw_w_up[layer], rw_w0[layer], rw_a_up[layer],
                                  rw_a0[layer], rw_g_up[layer], rw_k_k[layer], rw_k_a[layer],
                                  rw_r_k[layer], rw_gn_w[layer], rw_gn_b[layer], v_first, vres)
        y_ssm = mamba2_mix(p_ssm, ssm_conv_w[layer], ssm_conv_b[layer], ssm_dt_bias[layer],
                           ssm_a_log[layer], ssm_d[layer], ssm_norm_w[layer])
        y_ret = retention_mix(p_ret, positions)
        merged = None
        for i, y_b in enumerate((y_rw, y_ssm, y_ret)):
            gate = jax.nn.sigmoid(gate_logits[..., i * D_MODEL:(i + 1) * D_MODEL].astype(f32)).astype(act_dtype)
            term = gate * (y_b.astype(act_dtype) @ w_branch[layer, i])
            merged = term if merged is None else merged + term
        x = x + merged @ w_out[layer]
        h2 = rms_norm(x, norm2_w[layer])
        j = layer // 2
        if layer % 2 == 0:
            x = x + swiglu(h2, ffn_wg[j], ffn_wu[j], ffn_wd[j])
        else:
            x = x + moe_swiglu(h2, moe_router[j], moe_wg[j], moe_wu[j], moe_wd[j])
    return rms_norm(x, final_norm_w)


_drawn_inputs = setup_inputs


def setup_inputs(seed=0):
    import zlib

    import numpy as np

    out = dict(_drawn_inputs(seed))
    spreads = {}
    factors = {'rw_w_up': 7.274,
     'rw_gn_b': 5.008,
     'rw_v0': 9.352,
     'ssm_conv_b': 2.99,
     'rw_v_down': 3.203,
     'rw_v_up': 4.311}
    for name, (base, spread) in spreads.items():
        noise = np.random.default_rng([zlib.crc32(name.encode()), seed]).standard_normal(out[name].shape)
        drawn = base * np.exp(spread * noise) if base else spread * noise
        out[name] = jnp.asarray(drawn.astype(out[name].dtype))
    for name, factor in factors.items():
        out[name] = (out[name] * factor).astype(out[name].dtype)
    return out
```

```python
from contextlib import ExitStack

import numpy as np

import concourse.bass as bass
from concourse import mybir

ALU = mybir.AluOpType
ACT = mybir.ActivationFunctionType
AX = mybir.AxisListType
F32 = mybir.dt.float32
I32 = mybir.dt.int32
U32 = mybir.dt.uint32

P = 128
T = 256
TT = T // P
D = 1024
KT = D // P
W = 512
CT = W // P
HEADS, DH = 8, 64
DEPTH = 2
RW_COLS = 3 * W + 64 + 64 + 128
SSM_COLS = W + 1024 + 8
XBC_TILES = 8
TAPS = 4
D_FF, N_EXP, D_FFE = 2816, 8, 3584
FCH = D_FFE // W
RMS_EPS, GN_EPS = 1e-6, 64e-5
LEVELS = 6
SLOTS = 4
E_SLOTS = 7
RW_ORDER = (12, 4, 6, 0, 2, 8, 10)

CONSTS = [("ucent", 256), ("mask4", 512), ("ident", 128), ("merge", 128 * 7), ("rest", 128),
          ("ones", 128), ("headones", 128), ("swap", 128), ("cos", 256), ("sin", 256),
          ("decay", 1024), ("zeta", 8), ("xi", 8), ("headsel", 2), ("iota8", 8), ("slot", 128),
          ("neghalf", 1)]
COLS = [("norm1", 8), ("norm2", 8), ("mu", 14), ("kk", 4), ("ka", 4), ("a0", 4), ("rk", 4),
        ("v0", 4), ("ssmn", 4), ("convw", 32), ("convb", 8)]
ROWS = [("w0", 512), ("gnw", 512), ("gnb", 512), ("dtb", 8), ("alog", 8), ("dskip", 8)]


def offsets(table):
    at, out = 0, {}
    for name, n in table:
        out[name] = (at, n)
        at += n
    return out, at


CONST_AT, CONST_N = offsets(CONSTS)
COL_AT, COL_N = offsets(COLS)
ROW_AT, ROW_N = offsets(ROWS)


def constants():
    f = np.float32
    s, t = np.arange(P)[:, None], np.arange(P)[None, :]
    incl, strict = (s <= t), (s < t)
    mid = (s <= P // 2 - 1)
    rate = np.exp(-0.5)
    c = {}
    c["ucent"] = -rate * np.concatenate([strict.astype(np.float64) - mid, incl.astype(np.float64) - mid], 1)
    c["mask4"] = np.concatenate([strict, incl, strict, incl], 1)
    c["ident"] = np.eye(P)
    merge = []
    for b in (1, 2, 4, 8, 16, 32, 64):
        merge.append((s // (2 * b) == t // (2 * b)) & (s % (2 * b) < b) & (t % (2 * b) >= b))
    c["merge"] = np.concatenate(merge, 1)
    c["rest"] = (s > t)
    c["ones"] = np.ones((P, P))
    c["headones"] = (s // DH == t // DH)
    c["swap"] = (s == (t ^ 1))
    half = DH // 2
    inv = (np.float32(10000.0) ** (-np.arange(half, dtype=f) / f(half))).astype(f)
    ang = np.arange(T, dtype=f)[None, :] * inv[(np.arange(P) % DH) // 2][:, None]
    c["cos"] = np.cos(ang)
    c["sin"] = np.sin(ang) * np.where(np.arange(P) % 2 == 0, -1.0, 1.0)[:, None]
    lg = np.log1p(-np.exp2(-5.0 - np.arange(HEADS)))
    order = [0, 2, 4, 6, 1, 3, 5, 7]
    dec = [np.where(incl, np.exp(np.where(incl, t - s, 0) * lg[h]), 0.0) * DH ** -0.5 for h in order]
    c["decay"] = np.concatenate(dec, 1)
    c["zeta"] = np.exp((P - 1 - s) * lg[None, :]) * DH ** -0.5
    c["xi"] = np.exp((s + 1.0) * lg[None, :])
    c["headsel"] = (s // DH == np.arange(2)[None, :])
    c["iota8"] = np.broadcast_to(np.arange(8), (P, 8))
    c["slot"] = np.broadcast_to(np.arange(P), (P, P))
    c["neghalf"] = np.full((P, 1), -0.5)
    return np.ascontiguousarray(np.concatenate([np.asarray(c[n], f) for n, _ in CONSTS], 1))


PER = dict(sumsq=2, rstd=1, xn=2, hT=4,
           dt_raw=1, dt_na=1, dt_exp=1, dt_u=1, dt_ln=1, a_exp=1, dt_done=2, a_bcast=1, cs_sb=1, cs_exp=1,
           seg=16, segexp=4, gmat=4, cbm=2, xbc_raw=4, xbc_zero=1, conv=8, convsig=8, xbcT=8,
           xs_tok=2, b_tok=1, xdt=2, xdd=1, dxs=2, st_sb=1, yd_used=2, yo_used=1, zsig=2, zsilu=2,
           ssm_ss=2, ssm_rstd=2, yssm=2, yT=12,
           qraw=4, qcos=4, rot_used=4, qkT=4, rv=2, rgsig=2, rgate=2, scT=4, kz=1, kv_zero=1, kvbd=2,
           ry_used=2, rc_used=1, ret_ss=2, ret_rstd=2, yret=2,
           rw_raw=7, raw_zero=1, xm=14, xw_tanh=1, xg_sig=1, lwz=2, lw=2, gtok=2, a_sig=4, e1=4, e2=4,
           kksq=1, kkmax=2, kkr=1, rk=1, ar=2, kb=2, v_fin=1, vtok=2, bon=1, kb_tok=2,
           AT=16, XTi=4, Xi=4, LTm=24, P1=24, Xu=20, XTu=24, w_tok=2, u_tok=2, S_zero=1, Sbd=2,
           yraw=2, rw_ss=2, rw_rstd=2, yrw=2,
           gsig=12, brprod=12, merged=12, mT=4, xmix=4,
           vd=1, vsig=4, fgt=11, fhid=11, fsig=11, fdown=6, xffn=4, lg=1, sel=4, rank=2)
PARAMS = (5 * 16, 12 * 16)


def trunk(nc, t):
    ctx = ExitStack()
    with ctx:
        def sb(name, cols, dt=F32):
            return ctx.enter_context(nc.sbuf_tensor(name, [P, cols], dt))

        sems = {}

        def sem(name):
            if name not in sems:
                sems[name] = ctx.enter_context(nc.semaphore("s_" + name))
            return sems[name]

        counts = {}

        def up(ins, name):
            counts[name] = counts.get(name, 0) + 1
            return ins.then_inc(sem(name), 1)

        def need(eng, name, l, k):
            eng.wait_ge(sem(name), l * PER[name] + k)

        def own(eng, name):
            eng.wait_ge(sem(name), counts[name])

        X = sb("X", TT * D)[:, :].rearrange("p (t d) -> p t d", t=TT)
        xn = sb("xn", TT * D)[:, :].rearrange("p (t d) -> p t d", t=TT)
        hT = sb("hT", KT * T)[:, :].rearrange("p (k t) -> p k t", k=KT)
        slab = sb("slab", SLOTS * KT * W)[:, :].rearrange("p (s n) -> p s n", s=SLOTS)
        const = sb("const", CONST_N)
        pcol = sb("pcol", DEPTH * COL_N)
        prow = sb("prow", ROW_N)
        wa_up = sb("wa_up", W)
        g_up = sb("g_up", W)
        v_down = sb("v_down", CT * 32)[:, :].rearrange("p (c n) -> p c n", c=CT)
        v_up = sb("v_up", W)
        wdt = sb("wdt", KT * 8)[:, :].rearrange("p (k n) -> p k n", k=KT)
        router = sb("router", KT * 8)[:, :].rearrange("p (k n) -> p k n", k=KT)
        small = sb("small", 640)
        yT = sb("yT", 3 * CT * T)[:, :].rearrange("p (b c t) -> p b c t", b=3, c=CT)
        finw = yT[:, 0].rearrange("p c t -> p (c t)")
        vfirst = sb("vfirst", CT * T)[:, :].rearrange("p (c t) -> p c t", c=CT)
        KB = 256
        arena = sb("arena", 70 * KB)
        psum = [ctx.enter_context(nc.psum_tensor(f"bank{b}", [P, 512], F32)) for b in range(8)]

        def area(kb, cols):
            a = int(kb * KB)
            assert a + cols <= 70 * KB, (kb, cols)
            return arena[:, a:a + cols]

        def cst(name, i=0, n=None):
            a, m = CONST_AT[name]
            n = m if n is None else n
            return const[:, a + i * n:a + i * n + n]

        def col(l, name, i, n=1):
            a = l * COL_N + COL_AT[name][0] + i
            return pcol[:, a:a + n]

        def row(name):
            a, n = ROW_AT[name]
            return prow[:, a:a + n]

        def over(ap, n):
            return ap.unsqueeze(2).to_broadcast([ap.shape[0], ap.shape[1], n])

        def rep(ap, n):
            return ap.unsqueeze(1).to_broadcast([ap.shape[0], n, ap.shape[1]])

        small_at = [0]

        def sm(n):
            a = small_at[0]
            small_at[0] += n
            assert small_at[0] <= 640
            return small[:, a:a + n]

        ss, rs = sm(2), sm(2)
        dtr, dtm, dna, dte, dtu, dln = sm(16), sm(16), sm(16), sm(16), sm(16), sm(16)
        dd, dz, dq = sm(16), sm(16), sm(16)
        dt_tok, a_tok, a_neg, cs, ecs = sm(16), sm(16), sm(8), sm(24), sm(16)
        g2, g2r = sm(4), sm(4)
        r8, r8r = sm(16), sm(16)
        m8, v8, v8r = sm(16), sm(16), sm(16)
        bons, rec4, sS = sm(16), sm(4), sm(4)
        lg, mx8, idxf, oh1, oh2 = sm(16), sm(16), sm(16), sm(16), sm(16)
        ex, w12, gate8, sel8, pos8, flagf = sm(2), sm(4), sm(16), sm(16), sm(16), sm(8)
        cur = sm(8)
        idx8 = sb("idx8", 16, U32)
        flag = sb("flag", 1, I32)

        s_raw = area(0, 8 * 259).rearrange("p (c t) -> p c t", c=8)
        s_xbc = area(8.25, 2048).rearrange("p (c t) -> p c t", c=8)
        s_acc = area(16.25, 2048).rearrange("p (c t) -> p c t", c=8)
        s_sig = area(24.25, 2048).rearrange("p (c t) -> p c t", c=8)
        s_xs = area(32.25, 1024).rearrange("p (t n) -> p t n", t=TT)
        s_xdt = area(36.25, 1024).rearrange("p (t n) -> p t n", t=TT)
        s_xdd = area(40.25, 512)
        s_bt = area(42.25, 256)
        s_ab = area(43.25, 2048).rearrange("p (h n) -> p h n", h=16)
        s_L = area(51.25, 1024).rearrange("p (b h n) -> p b h n", b=2, h=4)
        s_G = area(55.25, 2048).rearrange("p (t h n) -> p t h n", t=TT, h=8)
        s_z = area(63.25, 1024).rearrange("p (t n) -> p t n", t=TT)
        s_st = area(67.25, 512)
        s_cb = area(0, 512).rearrange("p (t g n) -> p t g n", t=TT, g=2)
        s_y = area(24.25, 1024).rearrange("p (t n) -> p t n", t=TT)
        s_sq = area(28.25, 512)
        s_dx = area(2.25, 1024).rearrange("p (t n) -> p t n", t=TT)
        r_raw = area(0, 2048).rearrange("p (c t) -> p c t", c=8)
        r_qk = area(8, 2048).rearrange("p (c t) -> p c t", c=8)
        r_t = area(16, 512).rearrange("p (c t) -> p c t", c=2)
        r_v = area(18, 1024).rearrange("p (t n) -> p t n", t=TT)
        r_g = area(22, 1024).rearrange("p (t n) -> p t n", t=TT)
        r_sc = area(26, 2048).rearrange("p (t q i n) -> p t q i n", t=TT, q=2, i=4)
        r_kz = area(34, 512)
        r_kv = area(36, 512).rearrange("p (c n) -> p c n", c=CT)
        r_y = area(38, 1024).rearrange("p (t n) -> p t n", t=TT)
        r_sq = area(42, 512)
        w_raw = area(0, 14 * 257).rearrange("p (c t) -> p c t", c=14)
        w_ar = area(0, 2048).rearrange("p (c t s n) -> p c t s n", c=CT, t=TT, s=2)
        w_k = area(8, 1024).rearrange("p (c t) -> p c t", c=CT)
        w_b = area(12, 1024).rearrange("p (c t) -> p c t", c=CT)
        w_xm = area(16, 14 * 256).rearrange("p (c t) -> p c t", c=14)
        w_e1 = area(30, 2048).rearrange("p (c t s n) -> p c t s n", c=CT, t=TT, s=2)
        w_e2 = area(38, 1024).rearrange("p (c t) -> p c t", c=CT)
        w_a = area(42, 1024).rearrange("p (c t) -> p c t", c=CT)
        w_kk = area(46, 1024).rearrange("p (c t) -> p c t", c=CT)
        w_sq = area(50, 1024).rearrange("p (c t) -> p c t", c=CT)
        w_lw = area(54, 1024).rearrange("p (t n) -> p t n", t=TT)
        w_g = area(58, 1024).rearrange("p (t n) -> p t n", t=TT)
        w_vt = area(62, 1024).rearrange("p (t n) -> p t n", t=TT)
        w_S = area(66, 512).rearrange("p (c n) -> p c n", c=CT)
        w_vd = area(68, 256)
        w_AT = area(16, 4096).rearrange("p (h q n) -> p h q n", h=8, q=4)
        w_LT = area(32, 1024).rearrange("p (h n) -> p h n", h=8)
        w_X = area(36, 1024).rearrange("p (h n) -> p h n", h=8)
        w_XT = area(40, 1024).rearrange("p (h n) -> p h n", h=8)
        w_P1 = area(44, 1024).rearrange("p (h n) -> p h n", h=8)
        w_kt = area(48, 512)
        w_bt = area(50, 512)
        w_w = area(52, 512)
        w_u = area(54, 512)
        w_y = xn[:, 0, 0:512]
        w_t = xn[:, 0, 512:1024]
        w_o = xn[:, 1, :].rearrange("p (t n) -> p t n", t=TT)
        gates = area(0, 12 * 512).rearrange("p (i n) -> p i n", i=12)
        prod = area(24, 1024).rearrange("p (b n) -> p b n", b=2)
        f_s = area(0, 1024).rearrange("p (b n) -> p b n", b=2)
        f_h = area(4, 22 * T).rearrange("p (f t) -> p f t", f=22)
        e_P = area(0, 256).rearrange("p (t n) -> p t n", t=TT)
        e_G = area(1, 256).rearrange("p (t n) -> p t n", t=TT)
        e_GT = area(2, 256)
        e_x = hT[:, 0:4, :].rearrange("p c (t n) -> p (c t) n", t=TT)
        e_s = area(3, 1024).rearrange("p (b n) -> p b n", b=2)
        e_h = area(7, 1024).rearrange("p (b n) -> p b n", b=2)
        e_hT = area(11, 1024).rearrange("p (b f n) -> p b f n", b=2, f=4)
        e_y = area(15, 1024)
        e_slab = [slab[:, i, :] for i in range(SLOTS)] + [area(22 + 16 * i, KT * W) for i in range(E_SLOTS - SLOTS)]

        where, turn, left = {}, {"G": 0, "A": 0}, {}
        base = {"G": 0, "A": 4}
        filled = [0] * 8

        def open_bank(pe, pool, name, sig, l, k):
            b = base[pool] + turn[pool] % 4
            turn[pool] += 1
            if b in left:
                need(pe, *left[b])
            left[b] = (sig, l, k)
            filled[b] += 1
            where[name] = (b, filled[b])
            return psum[b]

        def full(mm, name):
            mm.then_inc(sem(f"full{where[name][0]}"), 1)

        def bank(eng, name):
            b, n = where[name]
            eng.wait_ge(sem(f"full{b}"), n)
            return psum[b]

        slabs, spent_by = [], {}

        def use_slab(pe, key):
            n = len(slabs)
            slabs.append(key)
            pe.wait_ge(sem(f"slab{n % SLOTS}"), 16 * (n // SLOTS + 1))
            return slab[:, n % SLOTS, :]

        def x_ready(eng, n):
            if n == 0:
                eng.wait_ge(sem("xin"), 16)
            elif n % 2:
                need(eng, "xmix", n // 2, 4)
            else:
                need(eng, "xffn", 0, 4)

        def overflow(eng, experts):
            eng.wait_ge(sem("e_flag"), 1)
            most = eng.value_load(flag[0:1, 0:1], min_val=0, max_val=T)
            with eng.If(most > P):
                experts(N_EXP)

        block = ctx.enter_context(nc.Block())

        @block.tensor
        def _(pe):
            mm, tr = nc.tensor.matmul, nc.tensor.transpose
            ident = cst("ident")

            def spent(n, name):
                spent_by[n] = (f"full{where[name][0]}", where[name][1])

            def norm(n):
                need(pe, "xn", n, 2)
                for j in range(4):
                    b = open_bank(pe, "G", ("xT", n, j), "hT", n, j + 1)
                    for i in range(2):
                        for tt in range(TT):
                            m = tr(b[:, i * T + tt * P:i * T + tt * P + P],
                                   xn[:, tt, (2 * j + i) * P:(2 * j + i + 1) * P], ident)
                    full(m, ("xT", n, j))
                need(pe, "hT", n, 4)

            def channel_pair(b, w, c0):
                for i in range(2):
                    for k in range(KT):
                        m = mm(b[:, i * T:(i + 1) * T], w[:, k, c0 + i * P:c0 + (i + 1) * P], hT[:, k, :],
                               start=k == 0, stop=k == KT - 1)
                return m

            def token_tile(b, w, tt):
                for k in range(KT):
                    m = mm(b[:, :], hT[:, k, tt * P:(tt + 1) * P], w[:, k, :], start=k == 0, stop=k == KT - 1)
                return m

            def view(s, cols=W):
                return s[:, 0:KT * cols].rearrange("p (k n) -> p k n", k=KT)

            def pairs(l, key, jobs):
                w = view(use_slab(pe, key), 256 if len(jobs) == 1 else W)
                for n, (name, sig, k) in enumerate(jobs):
                    b = open_bank(pe, "G", name, sig, l, k)
                    full(channel_pair(b, w, 2 * P * n), name)
                spent(len(slabs) - 1, name)

            def tiles(l, key, names, sig, k0):
                w = view(use_slab(pe, key))
                for tt in range(TT):
                    b = open_bank(pe, "G", names[tt], sig, l, k0 + tt + 1)
                    full(token_tile(b, w, tt), names[tt])
                spent(len(slabs) - 1, names[-1])

            def turn_y(l, i, src, sig, k):
                per = 4 if i == 1 else 1
                k0 = {1: 0, 2: 8, 0: 10}[i]
                for tt in range(TT):
                    need(pe, sig, l, tt + 1)
                    b = open_bank(pe, "A", ("yT", l, i, tt), "yT", l, k0 + per * (tt + 1))
                    for c in range(CT):
                        m = tr(b[:, c * P:(c + 1) * P], src[:, tt, c * P:(c + 1) * P], ident)
                    full(m, ("yT", l, i, tt))

            def ssm(l):
                pe.wait_ge(sem("params"), PARAMS[l])
                b = open_bank(pe, "G", ("dt", l), "dt_raw", l, 1)
                for tt in range(TT):
                    for k in range(KT):
                        m = mm(b[:, 8 * tt:8 * tt + 8], hT[:, k, tt * P:(tt + 1) * P], wdt[:, k, :],
                               start=k == 0, stop=k == KT - 1)
                full(m, ("dt", l))
                for s in range(2):
                    pairs(l, ("xbc", l, s), [(("xbc", l, 2 * s + j), "xbc_raw", 2 * s + j + 1) for j in range(2)])
                need(pe, "dt_done", l, 2)
                b = open_bank(pe, "A", ("cs", l), "cs_sb", l, 1)
                for i, (mask, tt) in enumerate((("incl", 0), ("incl", 1), ("rest", 0))):
                    lhs = cst("rest") if mask == "rest" else cst("mask4", 1, 128)
                    m = mm(b[:, 8 * i:8 * i + 8], lhs, a_tok[:, 8 * tt:8 * tt + 8], start=True, stop=True)
                full(m, ("cs", l))
                need(pe, "a_bcast", l, 1)
                for tt in range(TT):
                    for g in range(2):
                        b = open_bank(pe, "A", ("seg", l, tt, g), "seg", l, 4 * (2 * tt + g + 1))
                        for h in range(4):
                            m = mm(b[:, h * P:(h + 1) * P], s_ab[:, 8 * tt + 4 * g + h, :], cst("mask4", 1, 128),
                                   start=True, stop=True)
                        full(m, ("seg", l, tt, g))
                tiles(l, ("z", l), [("z", l, tt) for tt in range(TT)], "zsilu", 0)
                need(pe, "xbcT", l, 8)
                for tt in range(TT):
                    b = open_bank(pe, "A", ("cb", l, tt), "cbm", l, tt + 1)
                    for g in range(2):
                        m = mm(b[:, g * P:(g + 1) * P], s_xbc[:, 4 + g, tt * P:(tt + 1) * P],
                               s_xbc[:, 6 + g, tt * P:(tt + 1) * P], start=True, stop=True)
                    full(m, ("cb", l, tt))
                for tt in range(TT):
                    b = open_bank(pe, "A", ("xst", l, tt), "xs_tok", l, tt + 1)
                    for c in range(CT):
                        m = tr(b[:, c * P:(c + 1) * P], s_xbc[:, c, tt * P:(tt + 1) * P], ident)
                    full(m, ("xst", l, tt))
                b = open_bank(pe, "A", ("bt", l), "b_tok", l, 1)
                for g in range(2):
                    m = tr(b[:, g * P:(g + 1) * P], s_xbc[:, 4 + g, 0:P], ident)
                full(m, ("bt", l))
                need(pe, "xdd", l, 1)
                need(pe, "b_tok", l, 1)
                b = open_bank(pe, "A", ("st", l), "st_sb", l, 1)
                for g in range(2):
                    m = mm(b[:, g * T:(g + 1) * T], s_bt[:, g * P:(g + 1) * P], s_xdd[:, g * T:(g + 1) * T],
                           start=True, stop=True)
                full(m, ("st", l))
                for tt in range(TT):
                    need(pe, "gmat", l, 2 * tt + 2)
                    need(pe, "xdt", l, tt + 1)
                    b = open_bank(pe, "A", ("yd", l, tt), "yd_used", l, tt + 1)
                    for h in range(HEADS):
                        m = mm(b[:, h * DH:(h + 1) * DH], s_G[:, tt, h, :], s_xdt[:, tt, h * DH:(h + 1) * DH],
                               start=True, stop=True)
                    full(m, ("yd", l, tt))
                need(pe, "st_sb", l, 1)
                b = open_bank(pe, "A", ("yo", l), "yo_used", l, 1)
                for g in range(2):
                    m = mm(b[:, g * T:(g + 1) * T], s_xbc[:, 6 + g, P:T], s_st[:, g * T:(g + 1) * T],
                           start=True, stop=True)
                full(m, ("yo", l))
                turn_y(l, 1, s_y, "yssm", 0)

            def retention(l):
                for s in range(2):
                    pairs(l, ("rqk", l, s), [(("qk", l, 2 * s + j), "qraw", 2 * s + j + 1) for j in range(2)])
                for j in range(4):
                    need(pe, "qraw", l, j + 1)
                    b = open_bank(pe, "A", ("rot", l, j), "rot_used", l, j + 1)
                    full(mm(b[:, :], cst("swap"), r_raw[:, 2 * j:2 * j + 2, :], start=True, stop=True), ("rot", l, j))
                tiles(l, ("rv", l), [("rv", l, tt) for tt in range(TT)], "rv", 0)
                tiles(l, ("rg", l), [("rg", l, tt) for tt in range(TT)], "rgate", 0)
                need(pe, "qkT", l, 4)
                for tt in range(TT):
                    for q in range(2):
                        b = open_bank(pe, "A", ("sc", l, tt, q), "scT", l, 2 * tt + q + 1)
                        for i in range(4):
                            m = mm(b[:, i * P:(i + 1) * P], r_qk[64 * q:64 * q + 64, 4 + i, tt * P:(tt + 1) * P],
                                   r_qk[64 * q:64 * q + 64, i, tt * P:(tt + 1) * P], start=True, stop=True)
                        full(m, ("sc", l, tt, q))
                b = open_bank(pe, "A", ("kt", l), "kz", l, 1)
                for c in range(CT):
                    m = tr(b[:, c * P:(c + 1) * P], r_qk[:, 4 + c, 0:P], ident)
                full(m, ("kt", l))
                need(pe, "kz", l, 1)
                need(pe, "rv", l, 2)
                b = open_bank(pe, "A", ("kv", l), "kvbd", l, 2)
                for c in range(CT):
                    m = mm(b[:, c * P:(c + 1) * P], r_kz[:, c * P:(c + 1) * P], r_v[:, 0, c * P:(c + 1) * P],
                           start=True, stop=True)
                full(m, ("kv", l))
                for tt in range(TT):
                    need(pe, "scT", l, 2 * tt + 2)
                    b = open_bank(pe, "A", ("ry", l, tt), "ry_used", l, tt + 1)
                    for h in range(HEADS):
                        m = mm(b[:, h * DH:(h + 1) * DH], r_sc[:, tt, h % 2, h // 2, :],
                               r_v[:, tt, h * DH:(h + 1) * DH], start=True, stop=True)
                    full(m, ("ry", l, tt))
                need(pe, "kvbd", l, 2)
                b = open_bank(pe, "A", ("rc", l), "rc_used", l, 1)
                for c in range(CT):
                    m = mm(b[:, c * P:(c + 1) * P], r_qk[:, c, P:T], r_kv[:, c, :], start=True, stop=True)
                full(m, ("rc", l))
                turn_y(l, 2, r_y, "yret", 0)

            def rwkv(l):
                pairs(l, ("lora", l), [(("rw", l, 0), "rw_raw", 1)])
                for s in range(3):
                    pairs(l, (("rwk", "rwr", "rwv")[s], l),
                          [(("rw", l, 1 + 2 * s + j), "rw_raw", 2 + 2 * s + j) for j in range(2)])
                need(pe, "xw_tanh", l, 1)
                for tt in range(TT):
                    b = open_bank(pe, "A", ("lw", l, tt), "lwz", l, tt + 1)
                    full(mm(b[:, :], w_xm[0:64, 12, tt * P:(tt + 1) * P], wa_up[0:64, :], start=True, stop=True),
                         ("lw", l, tt))
                for j in range(2):
                    b = open_bank(pe, "A", ("a", l, j), "a_sig", l, 2 * j + 2)
                    for i in range(2):
                        c = 2 * j + i
                        m = mm(b[:, i * T:(i + 1) * T], wa_up[64:128, c * P:(c + 1) * P], w_xm[64:128, 12, :],
                               start=True, stop=True)
                    full(m, ("a", l, j))
                need(pe, "xg_sig", l, 1)
                for tt in range(TT):
                    b = open_bank(pe, "A", ("g", l, tt), "gtok", l, tt + 1)
                    full(mm(b[:, :], w_xm[:, 13, tt * P:(tt + 1) * P], g_up[:, :], start=True, stop=True), ("g", l, tt))
                need(pe, "kksq", l, 1)
                for j in range(2):
                    b = open_bank(pe, "A", ("kks", l, j), "kkmax", l, j + 1)
                    full(mm(b[:, :], cst("headones"), w_sq[:, 2 * j:2 * j + 2, :], start=True, stop=True),
                         ("kks", l, j))
                need(pe, "lw", l, 2)
                for c in range(CT):
                    b = open_bank(pe, "A", ("cum", l, c), "e2", l, c + 1)
                    for tt in range(TT):
                        m = mm(b[:, tt * T:(tt + 1) * T], w_lw[:, tt, c * P:(c + 1) * P], cst("ucent"),
                               start=True, stop=True)
                    full(m, ("cum", l, c))
                if l > 0:
                    need(pe, "xm", l, 14)
                    b = open_bank(pe, "A", ("vd", l), "vd", 0, 1)
                    for c in range(CT):
                        m = mm(b[0:32, 0:T], v_down[:, c, :], w_xm[:, 8 + c, :], start=c == 0, stop=c == CT - 1)
                    full(m, ("vd", l))
                    need(pe, "vd", 0, 1)
                    for j in range(2):
                        b = open_bank(pe, "A", ("vu", l, j), "vsig", 0, 2 * j + 2)
                        for i in range(2):
                            c = 2 * j + i
                            m = mm(b[:, i * T:(i + 1) * T], v_up[0:32, c * P:(c + 1) * P], w_vd[0:32, :],
                                   start=True, stop=True)
                        full(m, ("vu", l, j))
                need(pe, "v_fin", l, 1)
                for tt in range(TT):
                    b = open_bank(pe, "A", ("vT", l, tt), "vtok", l, tt + 1)
                    for c in range(CT):
                        m = tr(b[:, c * P:(c + 1) * P], w_xm[:, 8 + c, tt * P:(tt + 1) * P], ident)
                    full(m, ("vT", l, tt))
                need(pe, "rk", l, 1)
                b = open_bank(pe, "A", ("bon", l), "bon", l, 1)
                for tt in range(TT):
                    for c in range(CT):
                        m = mm(b[:, 8 * tt + 2 * c:8 * tt + 2 * c + 2], w_sq[:, c, tt * P:(tt + 1) * P], cst("headsel"),
                               start=True, stop=True)
                full(m, ("bon", l))
                need(pe, "kb", l, 2)
                for i, src in enumerate((w_k, w_b)):
                    b = open_bank(pe, "A", ("kbt", l, i), "kb_tok", l, i + 1)
                    for c in range(CT):
                        m = tr(b[:, c * P:(c + 1) * P], src[:, c, 0:P], ident)
                    full(m, ("kbt", l, i))
                need(pe, "ar", l, 2)
                for tt in range(TT):
                    core(l, tt)
                turn_y(l, 0, w_o, "yrw", 0)

            def core(l, tt):
                for h in range(HEADS):
                    c, p0 = h // 2, 64 * (h % 2)
                    b = open_bank(pe, "A", ("A", l, tt, h), "AT", l, 8 * tt + h + 1)
                    rhs = w_ar[p0:p0 + 64, c, tt, :, :]
                    mm(b[:, 0:256], w_b[p0:p0 + 64, c, tt * P:(tt + 1) * P], rhs, start=True, stop=True)
                    full(mm(b[:, 256:512], w_k[p0:p0 + 64, c, tt * P:(tt + 1) * P], rhs, start=True, stop=True),
                         ("A", l, tt, h))
                for g in range(2):
                    need(pe, "XTi", l, 2 * tt + g + 1)
                    b = open_bank(pe, "A", ("X0", l, tt, g), "Xi", l, 2 * tt + g + 1)
                    for i in range(4):
                        m = tr(b[:, i * P:(i + 1) * P], w_XT[:, 4 * g + i, :], ident)
                    full(m, ("X0", l, tt, g))
                for v in range(LEVELS):
                    for g in range(2):
                        need(pe, "LTm", l, 12 * tt + 2 * v + g + 1)
                        if v == 0:
                            need(pe, "Xi", l, 2 * tt + g + 1)
                        else:
                            need(pe, "Xu", l, 10 * tt + 2 * (v - 1) + g + 1)
                        b = open_bank(pe, "A", ("P1", l, tt, v, g), "P1", l, 12 * tt + 2 * v + g + 1)
                        for i in range(4):
                            m = mm(b[:, i * P:(i + 1) * P], w_LT[:, 4 * g + i, :], w_X[:, 4 * g + i, :],
                                   start=True, stop=True)
                        full(m, ("P1", l, tt, v, g))
                    for g in range(2):
                        need(pe, "P1", l, 12 * tt + 2 * v + g + 1)
                        if v > 0:
                            need(pe, "XTu", l, 12 * tt + 2 * (v - 1) + g + 1)
                        if v < LEVELS - 1:
                            b = open_bank(pe, "A", ("XU", l, tt, v, g), "Xu", l, 10 * tt + 2 * v + g + 1)
                            for i in range(4):
                                m = mm(b[:, i * P:(i + 1) * P], w_XT[:, 4 * g + i, :], w_P1[:, 4 * g + i, :],
                                       start=True, stop=True)
                            full(m, ("XU", l, tt, v, g))
                        b = open_bank(pe, "A", ("XTU", l, tt, v, g), "XTu", l, 12 * tt + 2 * v + g + 1)
                        for i in range(4):
                            m = mm(b[:, i * P:(i + 1) * P], w_P1[:, 4 * g + i, :], w_XT[:, 4 * g + i, :],
                                   start=True, stop=True)
                        full(m, ("XTU", l, tt, v, g))
                need(pe, "vtok", l, 2)

                def heads_product(name, sig, terms, state):
                    b = open_bank(pe, "A", (name, l, tt), sig, l, tt + 1)
                    for c in range(CT):
                        if tt:
                            mm(b[:, c * P:(c + 1) * P], w_ar[:, c, tt, state, :], w_S[:, c, :], start=True, stop=False,
                               skip_group_check=True)
                        for h in (2 * c, 2 * c + 1):
                            for i, (lhs, rhs) in enumerate(terms):
                                m = mm(b[:, h * DH:(h + 1) * DH], lhs(h), rhs(h), start=(tt == 0 and i == 0),
                                       stop=i == len(terms) - 1, skip_group_check=True)
                    full(m, (name, l, tt))

                if tt:
                    need(pe, "Sbd", l, 2)
                heads_product("w", "w_tok", [(lambda h: w_AT[:, h, 2, :], lambda h: w_vt[:, tt, h * DH:(h + 1) * DH])], 0)
                need(pe, "w_tok", l, tt + 1)
                need(pe, "XTu", l, 12 * tt + 12)
                b = open_bank(pe, "A", ("u", l, tt), "u_tok", l, tt + 1)
                for h in range(HEADS):
                    m = mm(b[:, h * DH:(h + 1) * DH], w_XT[:, h, :], w_w[:, h * DH:(h + 1) * DH], start=True, stop=True)
                full(m, ("u", l, tt))
                need(pe, "u_tok", l, tt + 1)
                heads_product("y", "yraw", [(lambda h: w_AT[:, h, 3, :], lambda h: w_vt[:, tt, h * DH:(h + 1) * DH]),
                                            (lambda h: w_AT[:, h, 1, :], lambda h: w_u[:, h * DH:(h + 1) * DH])], 1)
                if tt == 0:
                    need(pe, "kb_tok", l, 2)
                    b = open_bank(pe, "A", ("S", l), "Sbd", l, 2)
                    for c in range(CT):
                        s = slice(c * P, (c + 1) * P)
                        mm(b[:, s], w_kt[:, s], w_vt[:, 0, s], start=True, stop=False)
                        m = mm(b[:, s], w_bt[:, s], w_u[:, s], start=False, stop=True)
                    full(m, ("S", l))

            def merge(l):
                n = 0
                for i in range(3):
                    for half in range(2):
                        tiles(l, ("gate", l, i, half), [("gate", l, i, half, tt) for tt in range(TT)], "gsig", n)
                        n += 2
                n = 0
                for i in range(3):
                    w = use_slab(pe, ("branch", l, i)).rearrange("p (c n) -> p c n", c=CT)
                    need(pe, "yT", l, 12)
                    for half in range(2):
                        for tt in range(TT):
                            n += 1
                            b = open_bank(pe, "A", ("br", l, i, half, tt), "brprod", l, n)
                            for c in range(CT):
                                m = mm(b[:, :], yT[:, i, c, tt * P:(tt + 1) * P], w[:, c, half * W:(half + 1) * W],
                                       start=c == 0, stop=c == CT - 1)
                            full(m, ("br", l, i, half, tt))
                    spent(len(slabs) - 1, ("br", l, i, 1, 1))
                need(pe, "merged", l, 12)
                for j in range(4):
                    b = open_bank(pe, "G", ("mT", l, j), "mT", l, j + 1)
                    for i in range(2):
                        for tt in range(TT):
                            m = tr(b[:, i * T + tt * P:i * T + tt * P + P],
                                   xn[:, tt, (2 * j + i) * P:(2 * j + i + 1) * P], ident)
                    full(m, ("mT", l, j))
                need(pe, "mT", l, 4)
                for half in range(2):
                    tiles(l, ("out", l, half), [("out", l, half, tt) for tt in range(TT)], "xmix", 2 * half)

            def dense():
                nch, nft = -(-D_FF // W), D_FF // P
                acc = [psum[4 + i] for i in range(4)]
                for i in range(4):
                    need(pe, *left[4 + i])
                    left[4 + i] = ("xffn", 0, i + 1)

                def down(ch, n, w):
                    nf = min(4, nft - 4 * ch)
                    need(pe, "fhid", 0, 2 * ch + nf // 2)
                    for tt in range(TT):
                        for half in range(2):
                            for f in range(nf):
                                m = mm(acc[2 * tt + half][:, :], f_h[:, 4 * ch + f, tt * P:(tt + 1) * P],
                                       w[:, f, half * W:(half + 1) * W],
                                       start=ch == 0 and f == 0, stop=4 * ch + f == nft - 1)
                    up(m, "fdown")
                    spent_by[n] = ("fdown", ch + 1)

                waiting = None
                for ch in range(nch):
                    cols = min(W, D_FF - ch * W)
                    wg = view(use_slab(pe, ("fg", ch)), cols)
                    wu = view(use_slab(pe, ("fu", ch)), cols)
                    for j in range(cols // 256):
                        n = 2 * ch + j
                        for nm, w, sig in (("fg", wg, "fgt"), ("fu", wu, "fhid")):
                            b = open_bank(pe, "G", (nm, n), sig, 0, n + 1)
                            full(channel_pair(b, w, 2 * P * j), (nm, n))
                    spent(len(slabs) - 2, ("fg", n))
                    spent(len(slabs) - 1, ("fu", n))
                    if waiting:
                        down(*waiting)
                    w = use_slab(pe, ("fd", ch)).rearrange("p (f n) -> p f n", f=4)
                    waiting = (ch, len(slabs) - 1, w)
                down(*waiting)

            def route():
                b = open_bank(pe, "G", ("route",), "lg", 0, 1)
                pe.wait_ge(sem("router"), 16)
                for tt in range(TT):
                    for k in range(KT):
                        m = mm(b[:, 8 * tt:8 * tt + 8], hT[:, k, tt * P:(tt + 1) * P], router[:, k, :],
                               start=k == 0, stop=k == KT - 1)
                full(m, ("route",))
                need(pe, "sel", 0, 4)
                strict = cst("mask4", 0, 128)
                b = open_bank(pe, "G", ("rank",), "rank", 0, 2)
                mm(b[:, 0:8], strict, sel8[:, 0:8], start=True, stop=True)
                mm(b[:, 8:16], cst("ones"), sel8[:, 0:8], start=True, stop=False)
                mm(b[:, 8:16], strict, sel8[:, 8:16], start=False, stop=True)
                mm(b[:, 16:24], cst("ones"), sel8[:, 0:8], start=True, stop=False)
                full(mm(b[:, 16:24], cst("ones"), sel8[:, 8:16], start=False, stop=True), ("rank",))

            def experts(n0):
                with pe.Fori(0, N_EXP) as e0:
                    e = e0 + n0
                    pe.wait_ge(sem("e_onehot"), 4 * e + 4)
                    for j in range(2):
                        for i in range(4):
                            for tt in range(TT):
                                m = mm(psum[j][:, i * P:(i + 1) * P], xn[:, tt, (4 * j + i) * P:(4 * j + i + 1) * P],
                                       e_P[:, tt, :], start=tt == 0, stop=tt == TT - 1)
                        up(m, "e_gather")
                    for tt in range(TT):
                        m = tr(psum[2][:, tt * P:(tt + 1) * P], e_G[:, tt, :], ident)
                    up(m, "e_gather")
                    pe.wait_ge(sem("e_x"), 2 * e + 2)
                    pe.wait_ge(sem("e_gt"), e + 1)

                    def slab_of(i):
                        pe.wait_ge(sem(f"eslab{i % E_SLOTS}"), 16 * (3 * e + i // E_SLOTS + 1))
                        return e_slab[i % E_SLOTS]

                    def down(ch):
                        pe.wait_ge(sem("e_hid"), 7 * e + ch + 1)
                        for f in range(4):
                            m = tr(psum[6 + ch % 2][:, f * P:(f + 1) * P], e_h[:, ch % 2, f * P:(f + 1) * P], ident)
                        up(m, "e_turn")
                        pe.wait_ge(sem("e_hT"), 7 * e + ch + 1)
                        w = slab_of(3 * ch + 2).rearrange("p (f n) -> p f n", f=4)
                        for half in range(2):
                            for f in range(4):
                                m = mm(psum[4 + half][:, :], e_hT[:, ch % 2, f, :], w[:, f, half * W:(half + 1) * W],
                                       start=ch == 0 and f == 0, stop=ch == FCH - 1 and f == 3)
                        up(m, "e_down")

                    for ch in range(FCH):
                        for i in range(2):
                            w = view(slab_of(3 * ch + i))
                            if ch >= 2:
                                pe.wait_ge(sem("e_hid"), 7 * e + ch - 1)
                            for k in range(KT):
                                m = mm(psum[2 * (ch % 2) + i][:, :], e_x[:, k, :], w[:, k, :],
                                       start=k == 0, stop=k == KT - 1)
                            up(m, "e_up")
                        if ch:
                            down(ch - 1)
                    down(FCH - 1)
                    pe.wait_ge(sem("e_y"), 2 * e + 2)
                    for tt in range(TT):
                        for half in range(2):
                            m = mm(psum[2 * tt + half][:, :], e_GT[:, tt * P:(tt + 1) * P],
                                   e_y[:, half * W:(half + 1) * W], start=True, stop=True)
                            up(m, "e_comb")
                    pe.wait_ge(sem("e_add"), 4 * e + 4)

            pe.wait_ge(sem("const"), 16)
            for l in range(DEPTH):
                norm(2 * l)
                ssm(l)
                retention(l)
                rwkv(l)
                merge(l)
                norm(2 * l + 1)
                if l == 0:
                    dense()
                else:
                    route()
            need(pe, "rank", 0, 2)
            experts(0)
            overflow(pe, experts)

        @block.sync
        def _(sp):
            w_in = t["w_in"]
            rwc, ssc = 0, RW_COLS
            ret = RW_COLS + SSM_COLS
            gat = ret + 4 * W

            def src(key):
                k, l = key[0], key[1]
                if k in ("lora", "rwk", "rwr", "rwv", "xbc", "z", "rqk", "rv", "rg", "gate"):
                    c0 = {"lora": 3 * W, "rwk": W, "rwr": 0, "rwv": 2 * W, "z": ssc,
                          "rv": ret + 2 * W, "rg": ret + 3 * W}.get(k)
                    if k == "xbc":
                        c0 = ssc + W + key[2] * W
                    if k == "rqk":
                        c0 = ret + key[2] * W
                    if k == "gate":
                        c0 = gat + (2 * key[2] + key[3]) * W
                    n = 256 if k == "lora" else W
                    return w_in[l, :, c0:c0 + n].rearrange("(k p) n -> p k n", p=P), KT, n
                if k == "branch":
                    return t["w_branch"][l, key[2]].rearrange("(c p) n -> p c n", p=P), CT, D
                if k == "out":
                    return t["w_out"][l, :, key[2] * W:(key[2] + 1) * W].rearrange("(k p) n -> p k n", p=P), KT, W
                ch = key[1]
                if k in ("fg", "fu"):
                    n = min(W, D_FF - ch * W)
                    w = t["ffn_wg" if k == "fg" else "ffn_wu"]
                    return w[0, :, ch * W:ch * W + n].rearrange("(k p) n -> p k n", p=P), KT, n
                nf = min(4, 22 - 4 * ch)
                return t["ffn_wd"][0, ch * W:ch * W + nf * P, :].rearrange("(f p) n -> p f n", p=P), nf, D

            sp.dma_start(const[:, :], t["const"]).then_inc(sem("const"), 16)
            sp.dma_start(X, t["x"][0].rearrange("(t p) d -> p t d", p=P)).then_inc(sem("xin"), 16)
            sp.dma_start(pcol[:, :].rearrange("p (l n) -> p l n", l=DEPTH), t["pcol"].rearrange("l p n -> p l n"))\
                .then_inc(sem("pcol"), 16)
            for n, key in enumerate(slabs):
                if n >= SLOTS:
                    name, value = spent_by[n - SLOTS]
                    sp.wait_ge(sem(name), value)
                s, k, c = src(key)
                sp.dma_start(slab[:, n % SLOTS, 0:k * c].rearrange("p (k n) -> p k n", k=k), s)\
                    .then_inc(sem(f"slab{n % SLOTS}"), 16)

            def expert_slab(n0, e0, i, wait):
                ch, kind = i // 3, i % 3
                for name, value in wait:
                    sp.wait_ge(sem(name), value)
                s = t[("moe_wg", "moe_wu", "moe_wd")[kind]][0, bass.ds(e0, 1)]
                s = s[:, :, ch * W:(ch + 1) * W] if kind < 2 else s[:, ch * W:(ch + 1) * W, :]
                s = s.rearrange("e (k p) n -> p (e k) n", p=P)
                sp.dma_start(e_slab[i % E_SLOTS].rearrange("p (k n) -> p k n", k=KT if kind < 2 else 4), s)\
                    .then_inc(sem(f"eslab{i % E_SLOTS}"), 16)

            def read(e, i):
                ch, kind = i // 3, i % 3
                return [("e_up", 14 * e + 2 * ch + kind + 1) if kind < 2 else ("e_down", 7 * e + ch + 1)]

            def experts(n0):
                for i in range(E_SLOTS):
                    if n0:
                        wait = read(n0 - 1, 3 * FCH - E_SLOTS + i)
                    elif i < SLOTS:
                        wait = [spent_by[max(n for n in spent_by if n % SLOTS == i)]]
                    else:
                        wait = [("brprod", DEPTH * PER["brprod"]), ("merged", DEPTH * PER["merged"])]
                    expert_slab(n0, 0, i, wait)
                with sp.Fori(0, N_EXP - 1) as e0:
                    e = e0 + n0
                    for i in range(E_SLOTS, 3 * FCH):
                        expert_slab(n0, e0, i, read(e, i - E_SLOTS))
                    for i in range(E_SLOTS):
                        expert_slab(n0, e0 + 1, i, read(e, 3 * FCH - E_SLOTS + i))
                for i in range(E_SLOTS, 3 * FCH):
                    expert_slab(n0, N_EXP - 1, i, read(n0 + N_EXP - 1, i - E_SLOTS))

            experts(0)
            overflow(sp, experts)
            sp.wait_ge(sem("normed"), 2)
            sp.dma_start(t["out"][0].rearrange("(t p) d -> p t d", p=P), xn).then_inc(sem("stored"), 16)
            sp.wait_ge(sem("stored"), 16)

        @block.scalar
        def _(act):
            A, copy, mul = nc.scalar.activation, nc.scalar.copy, nc.scalar.mul

            def params(l):
                if l:
                    need(act, "brprod", l - 1, PER["brprod"])
                for dst, s in ((prow[:, :], t["prow"][l:l + 1, :].partition_broadcast(P)),
                               (wa_up[0:64, :], t["rw_w_up"][l]), (wa_up[64:128, :], t["rw_a_up"][l]),
                               (g_up[:, :], t["rw_g_up"][l]),
                               (wdt, t["w_in"][l, :, RW_COLS + SSM_COLS - 8:RW_COLS + SSM_COLS]
                                .rearrange("(k p) n -> p k n", p=P))):
                    act.dma_start(dst, s).then_inc(sem("params"), 16)
                if l:
                    act.dma_start(v_down, t["rw_v_down"][l - 1].rearrange("(c p) n -> p c n", p=P))\
                        .then_inc(sem("params"), 16)
                    act.dma_start(v_up[0:32, :], t["rw_v_up"][l - 1]).then_inc(sem("params"), 16)

            def norm(n):
                x_ready(act, n)
                for tt in range(TT):
                    up(A(xn[:, tt, :], X[:, tt, :], ACT.Square, accum_out=ss[:, tt:tt + 1]), "sumsq")
                need(act, "rstd", n, 1)
                for tt in range(TT):
                    up(mul(xn[:, tt, :], X[:, tt, :], rs[:, tt:tt + 1]), "xn")

            def turn_y(l, i):
                for tt in range(TT):
                    b = bank(act, ("yT", l, i, tt))
                    if i == 1:
                        for c in range(CT):
                            up(mul(yT[:, i, c, tt * P:(tt + 1) * P], b[:, c * P:(c + 1) * P], col(l, "ssmn", c)), "yT")
                    else:
                        up(copy(yT[:, i, :, tt * P:(tt + 1) * P], b[:, :].rearrange("p (c n) -> p c n", c=CT)), "yT")

            def ssm(l):
                act.wait_ge(sem("params"), PARAMS[l])
                up(A(a_neg, row("alog"), ACT.Exp), "a_exp")
                need(act, "dt_na", l, 1)
                up(A(dte, dna, ACT.Exp), "dt_exp")
                need(act, "dt_u", l, 1)
                up(A(dln, dtu, ACT.Ln), "dt_ln")
                need(act, "xbc_zero", l, 1)
                for j in range(4):
                    b = bank(act, ("xbc", l, j))
                    up(copy(s_raw[:, 2 * j:2 * j + 2, 3:3 + T], b[:, :].rearrange("p (c t) -> p c t", c=2)), "xbc_raw")
                for c in range(XBC_TILES):
                    need(act, "conv", l, c + 1)
                    up(A(s_sig[:, c, :], s_acc[:, c, :], ACT.Sigmoid, bias=col(l, "convb", c)), "convsig")
                for tt in range(TT):
                    b = bank(act, ("z", l, tt))
                    up(A(s_z[:, tt, :], b[:, :], ACT.Sigmoid), "zsig")
                need(act, "cs_sb", l, 1)
                up(A(ecs, cs[:, 8:24], ACT.Exp), "cs_exp")

                def decay(q):
                    need(act, "seg", l, 4 * q + 4)
                    up(A(s_L[:, q % 2], s_L[:, q % 2], ACT.Exp), "segexp")

                decay(0)
                decay(1)
                for tt in range(TT):
                    b = bank(act, ("xst", l, tt))
                    up(copy(s_xs[:, tt, :], b[:, :]), "xs_tok")
                b = bank(act, ("bt", l))
                up(copy(s_bt, b[:, 0:T]), "b_tok")
                decay(2)
                decay(3)
                b = bank(act, ("st", l))
                up(copy(s_st, b[:, :]), "st_sb")
                turn_y(l, 1)

            def retention(l):
                for j in range(4):
                    b = bank(act, ("qk", l, j))
                    up(copy(r_raw[:, 2 * j:2 * j + 2, :], b[:, :].rearrange("p (c t) -> p c t", c=2)), "qraw")
                for tt in range(TT):
                    b = bank(act, ("rv", l, tt))
                    up(copy(r_v[:, tt, :], b[:, :]), "rv")
                for tt in range(TT):
                    b = bank(act, ("rg", l, tt))
                    up(A(r_g[:, tt, :], b[:, :], ACT.Sigmoid), "rgsig")
                need(act, "kv_zero", l, 1)
                b = bank(act, ("kv", l))[:, :].rearrange("p (c n) -> p c n", c=CT)
                for q in range(2):
                    s = slice(64 * q, 64 * q + 64)
                    up(copy(r_kv[s, :, s], b[s, :, s]), "kvbd")
                turn_y(l, 2)

            def rwkv(l):
                need(act, "raw_zero", l, 1)
                for j in range(7):
                    b = bank(act, ("rw", l, j))
                    c = RW_ORDER[j]
                    up(copy(w_raw[:, c:c + 2, 1:1 + T], b[:, :].rearrange("p (c t) -> p c t", c=2)), "rw_raw")
                    if j == 2:
                        need(act, "xm", l, 2)
                        up(A(w_xm[0:64, 12, :], w_xm[0:64, 12, :], ACT.Tanh), "xw_tanh")
                        up(A(w_xm[:, 13, :], w_xm[:, 13, :], ACT.Sigmoid), "xg_sig")
                for tt in range(TT):
                    need(act, "lwz", l, tt + 1)
                    up(A(w_lw[:, tt, :], w_lw[:, tt, :], ACT.Sigmoid), "lw")
                for j in range(2):
                    b = bank(act, ("a", l, j))
                    for i in range(2):
                        c = 2 * j + i
                        up(A(w_a[:, c, :], b[:, i * T:(i + 1) * T], ACT.Sigmoid, bias=col(l, "a0", c)), "a_sig")
                for tt in range(TT):
                    b = bank(act, ("g", l, tt))
                    up(copy(w_g[:, tt, :], b[:, :]), "gtok")
                need(act, "kkmax", l, 2)
                up(A(w_sq, w_sq, ACT.Sqrt), "kkr")
                for c in range(CT):
                    b = bank(act, ("cum", l, c))
                    up(A(w_e1[:, c], b[:, :].rearrange("p (t s n) -> p t s n", t=TT, s=2), ACT.Exp), "e1")
                    up(A(w_e2[:, c, :].rearrange("p (t n) -> p t n", t=TT),
                         b[:, :].rearrange("p (t s n) -> p t s n", t=TT, s=2)[:, :, 1, :], ACT.Exp, scale=-1.0), "e2")
                if l > 0:
                    b = bank(act, ("vd", l))
                    up(copy(w_vd[0:32, :], b[0:32, 0:T]), "vd")
                    need(act, "kb", l, 2)
                    for j in range(2):
                        b = bank(act, ("vu", l, j))
                        for i in range(2):
                            c = 2 * j + i
                            up(A(w_a[:, c, :], b[:, i * T:(i + 1) * T], ACT.Sigmoid, bias=col(l, "v0", c)), "vsig")
                for tt in range(TT):
                    b = bank(act, ("vT", l, tt))
                    up(copy(w_vt[:, tt, :], b[:, :]), "vtok")
                for i, dst in enumerate((w_kt, w_bt)):
                    b = bank(act, ("kbt", l, i))
                    up(copy(dst, b[:, :]), "kb_tok")
                for tt in range(TT):
                    for g in range(2):
                        b = bank(act, ("X0", l, tt, g))
                        up(copy(w_X[:, 4 * g:4 * g + 4, :], b[:, :].rearrange("p (h n) -> p h n", h=4)), "Xi")
                    for v in range(LEVELS):
                        for g in range(2):
                            b = bank(act, ("P1", l, tt, v, g))
                            up(copy(w_P1[:, 4 * g:4 * g + 4, :], b[:, :].rearrange("p (h n) -> p h n", h=4)), "P1")
                    b = bank(act, ("w", l, tt))
                    up(copy(w_w, b[:, :]), "w_tok")
                    b = bank(act, ("u", l, tt))
                    up(copy(w_u, b[:, :]), "u_tok")
                    b = bank(act, ("y", l, tt))
                    up(copy(w_y, b[:, :]), "yraw")
                turn_y(l, 0)

            def merge(l):
                n = 0
                for i in range(3):
                    for half in range(2):
                        for tt in range(TT):
                            b = bank(act, ("gate", l, i, half, tt))
                            up(A(gates[:, n, :], b[:, :], ACT.Sigmoid), "gsig")
                            n += 1

            def dense():
                for n in range(D_FF // 256):
                    if n >= 2:
                        need(act, "fhid", 0, n - 1)
                    b = bank(act, ("fg", n))
                    up(A(f_s[:, n % 2, :], b[:, :], ACT.Sigmoid), "fsig")

            def experts(n0):
                with act.Fori(0, N_EXP) as e0:
                    e = e0 + n0
                    act.wait_ge(sem("e_gather"), 3 * e + 3)
                    up(copy(e_GT, psum[2][:, 0:T]), "e_gt")

                    def hidden(ch):
                        act.wait_ge(sem("e_turn"), 7 * e + ch + 1)
                        up(copy(e_hT[:, ch % 2], psum[6 + ch % 2][:, :].rearrange("p (f n) -> p f n", f=4)), "e_hT")

                    for ch in range(FCH):
                        act.wait_ge(sem("e_up"), 14 * e + 2 * ch + 1)
                        up(A(e_s[:, ch % 2, :], psum[2 * (ch % 2)][:, :], ACT.Sigmoid), "e_sig")
                        if ch:
                            hidden(ch - 1)
                    hidden(FCH - 1)
                    act.wait_ge(sem("e_down"), 7 * e + 7)
                    for half in range(2):
                        up(copy(e_y[:, half * W:(half + 1) * W], psum[4 + half][:, :]), "e_y")

            act.dma_start(router, t["moe_router"][0].rearrange("(k p) n -> p k n", p=P)).then_inc(sem("router"), 16)
            act.wait_ge(sem("pcol"), 16)
            for l in range(DEPTH):
                params(l)
                norm(2 * l)
                ssm(l)
                retention(l)
                rwkv(l)
                merge(l)
                norm(2 * l + 1)
                if l == 0:
                    dense()
            need(act, "brprod", DEPTH - 1, PER["brprod"])
            act.dma_start(finw, t["final_norm_w"].rearrange("(a d) -> a d", a=1).partition_broadcast(P))\
                .then_inc(sem("finw"), 16)
            for tt in range(TT):
                act.wait_ge(sem("top"), tt + 1)
                up(A(ex[:, tt:tt + 1], ex[:, tt:tt + 1], ACT.Exp), "topexp")
            experts(0)
            overflow(act, experts)
            act.wait_ge(sem("x_final"), 1)
            for tt in range(TT):
                up(A(xn[:, tt, :], X[:, tt, :], ACT.Square, accum_out=ss[:, tt:tt + 1]), "sumsq")

        @block.vector
        def _(dve):
            V = nc.vector
            TTo, TS, STT = V.tensor_tensor, V.tensor_scalar, V.scalar_tensor_tensor

            def step(ins):
                up(ins, "dve_step")
                own(dve, "dve_step")

            def norm(l, n, w):
                for j in range(4):
                    b = bank(dve, ("xT", n, j))
                    up(TTo(hT[:, 2 * j:2 * j + 2, :], b[:, :].rearrange("p (c t) -> p c t", c=2),
                           over(col(l, w, 2 * j, 2), T), ALU.mult), "hT")

            def ssm(l):
                dve.wait_ge(sem("params"), PARAMS[l])
                b = bank(dve, ("dt", l))
                up(TTo(dtr.rearrange("p (t h) -> p t h", t=TT), b[:, 0:16].rearrange("p (t h) -> p t h", t=TT),
                       rep(row("dtb"), TT), ALU.add), "dt_raw")
                own(dve, "dt_raw")
                up(STT(dna, dtr, -1.0, dtr, ALU.mult, ALU.min), "dt_na")
                up(TS(dtm, dtr, 0.0, None, ALU.max), "dve_step")
                need(dve, "dt_exp", l, 1)
                up(TS(dtu, dte, 1.0, None, ALU.add), "dt_u")
                own(dve, "dt_u")
                step(TS(dd, dtu, -1.0, None, ALU.add))
                up(TS(dz, dd, 0.0, None, ALU.is_equal), "dve_step")
                step(TS(dd, dd, 1e-30, None, ALU.max))
                step(V.reciprocal(dd, dd))
                step(TTo(dq, dte, dd, ALU.mult))
                need(dve, "dt_ln", l, 1)
                step(TTo(dq, dq, dln, ALU.mult))
                step(TTo(dz, dz, dte, ALU.mult))
                step(TTo(dq, dq, dz, ALU.add))
                up(TTo(dt_tok, dtm, dq, ALU.add), "dt_done")
                own(dve, "dt_done")
                need(dve, "a_exp", l, 1)
                up(STT(a_tok.rearrange("p (t h) -> p t h", t=TT), dt_tok.rearrange("p (t h) -> p t h", t=TT), -1.0,
                       rep(a_neg, TT), ALU.mult, ALU.mult), "dt_done")
                for j in range(4):
                    need(dve, "xbc_raw", l, j + 1)
                    for k in range(TAPS):
                        for c in (2 * j, 2 * j + 1):
                            w = col(l, "convw", c * TAPS + k)
                            if k == 0:
                                ins = TS(s_acc[:, c, :], s_raw[:, c, 0:T], w, None, ALU.mult)
                            else:
                                ins = STT(s_acc[:, c, :], s_raw[:, c, k:k + T], w, s_acc[:, c, :], ALU.mult, ALU.add)
                            up(ins, "conv" if k == TAPS - 1 else "dve_step")
                        own(dve, "conv" if k == TAPS - 1 else "dve_step")
                for c in range(XBC_TILES):
                    need(dve, "convsig", l, c + 1)
                    up(STT(s_xbc[:, c, :], s_acc[:, c, :], col(l, "convb", c), s_sig[:, c, :], ALU.add, ALU.mult), "xbcT")
                own(dve, "xbcT")
                b = bank(dve, ("cs", l))
                up(V.tensor_copy(cs, b[:, 0:24]), "cs_sb")
                own(dve, "cs_sb")

                def segment(q):
                    tt, g = q // 2, q % 2
                    b = bank(dve, ("seg", l, tt, g))
                    for h in range(4):
                        up(TS(s_L[:, q % 2, h, :], b[:, h * P:(h + 1) * P], cs[:, 8 * tt + 4 * g + h:8 * tt + 4 * g + h + 1],
                              0.0, ALU.subtract, ALU.min), "seg")

                def masked(tt):
                    b = bank(dve, ("cb", l, tt))
                    up(TTo(s_cb[:, tt], b[:, 0:256].rearrange("p (g n) -> p g n", g=2), rep(cst("mask4", 1, 128), 2),
                           ALU.mult), "cbm")
                    own(dve, "cbm")

                def weights(q):
                    tt, g = q // 2, q % 2
                    need(dve, "segexp", l, q + 1)
                    up(TTo(s_G[:, tt, 4 * g:4 * g + 4, :], s_L[:, q % 2], rep(s_cb[:, tt, g, :], 4), ALU.mult), "gmat")
                    own(dve, "gmat")

                for tt in range(TT):
                    segment(2 * tt)
                    segment(2 * tt + 1)
                    masked(tt)
                    weights(2 * tt)
                    weights(2 * tt + 1)
                for tt in range(TT):
                    need(dve, "zsig", l, tt + 1)
                    up(TTo(s_z[:, tt, :], s_z[:, tt, :], bank(dve, ("z", l, tt))[:, :], ALU.mult), "zsilu")
                own(dve, "zsilu")
                for tt in range(TT):
                    y = s_y[:, tt, :]
                    if tt:
                        b = bank(dve, ("yo", l))
                        up(TTo(s_sq.rearrange("p (h n) -> p h n", h=8), b[:, :].rearrange("p (h n) -> p h n", h=8),
                               over(ecs[:, 0:8], DH), ALU.mult), "yo_used")
                        own(dve, "yo_used")
                    need(dve, "dxs", l, tt + 1)
                    up(TTo(y, s_dx[:, tt, :], bank(dve, ("yd", l, tt))[:, :], ALU.add), "yd_used")
                    own(dve, "yd_used")
                    if tt:
                        step(TTo(y, y, s_sq, ALU.add))
                    step(TTo(y, y, s_z[:, tt, :], ALU.mult))
                    step(TTo(s_sq, y, y, ALU.mult))
                    up(V.tensor_reduce(g2[:, 0:2], s_sq.rearrange("p (g n) -> p g n", g=2), AX.X, ALU.add), "ssm_ss")
                    need(dve, "ssm_rstd", l, tt + 1)
                    up(TTo(y.rearrange("p (g n) -> p g n", g=2), y.rearrange("p (g n) -> p g n", g=2),
                           over(g2r[:, 0:2], 256), ALU.mult), "yssm")

            def retention(l):
                for j in range(4):
                    b = bank(dve, ("rot", l, j))
                    up(TTo(r_t, b[:, :].rearrange("p (c t) -> p c t", c=2), rep(cst("sin"), 2), ALU.mult), "rot_used")
                    own(dve, "rot_used")
                    need(dve, "qcos", l, j + 1)
                    up(TTo(r_qk[:, 2 * j:2 * j + 2, :], r_qk[:, 2 * j:2 * j + 2, :], r_t, ALU.add), "qkT")
                    own(dve, "qkT")
                for tt in range(TT):
                    need(dve, "rgsig", l, tt + 1)
                    up(TTo(r_g[:, tt, :], r_g[:, tt, :], bank(dve, ("rg", l, tt))[:, :], ALU.mult), "rgate")
                for tt in range(TT):
                    for q in range(2):
                        b = bank(dve, ("sc", l, tt, q))
                        up(TTo(r_sc[:, tt, q], b[:, :].rearrange("p (i n) -> p i n", i=4),
                               cst("decay", q, 512).rearrange("p (i n) -> p i n", i=4), ALU.mult), "scT")
                b = bank(dve, ("kt", l))
                up(TTo(r_kz.rearrange("p (h n) -> p h n", h=8), b[:, :].rearrange("p (h n) -> p h n", h=8),
                       over(cst("zeta"), DH), ALU.mult), "kz")
                for tt in range(TT):
                    y = r_y[:, tt, :]
                    yh = y.rearrange("p (h n) -> p h n", h=8)
                    if tt == 0:
                        up(V.tensor_copy(y, bank(dve, ("ry", l, 0))[:, :]), "ry_used")
                        own(dve, "ry_used")
                    else:
                        b = bank(dve, ("rc", l))
                        up(TTo(yh, b[:, :].rearrange("p (h n) -> p h n", h=8), over(cst("xi"), DH), ALU.mult), "rc_used")
                        own(dve, "rc_used")
                        up(TTo(y, y, bank(dve, ("ry", l, 1))[:, :], ALU.add), "ry_used")
                        own(dve, "ry_used")
                    step(TTo(r_sq, y, y, ALU.mult))
                    up(V.tensor_reduce(r8[:, 0:8], r_sq.rearrange("p (h n) -> p h n", h=8), AX.X, ALU.add), "ret_ss")
                    need(dve, "ret_rstd", l, tt + 1)
                    step(TTo(yh, yh, over(r8r[:, 0:8], DH), ALU.mult))
                    up(TTo(y, y, r_g[:, tt, :], ALU.mult), "yret")

            def rwkv(l):
                def c1024(ap):
                    return ap.rearrange("p c t -> p (c t)")

                def tile_pair(j):
                    c = RW_ORDER[j]
                    need(dve, "rw_raw", l, j + 1)
                    d = w_sq[:, 2 * (j % 2):2 * (j % 2) + 2, :]
                    step(TTo(d, w_raw[:, c:c + 2, 0:T], w_raw[:, c:c + 2, 1:1 + T], ALU.subtract))
                    for i in range(2):
                        up(STT(w_xm[:, c + i, :], d[:, i, :], col(l, "mu", c + i), w_raw[:, c + i, 1:1 + T],
                               ALU.mult, ALU.add), "xm")

                for j in range(5):
                    tile_pair(j)
                for tt in range(TT):
                    b = bank(dve, ("lw", l, tt))
                    up(TTo(w_lw[:, tt, :], b[:, :], row("w0"), ALU.add), "lwz")
                tile_pair(5)
                tile_pair(6)
                own(dve, "xm")
                kk, sq, k = w_kk, w_sq, w_xm[:, 4:8, :]
                step(TTo(kk, k, over(col(l, "kk", 0, 4), T), ALU.mult))
                up(TTo(sq, kk, kk, ALU.mult), "kksq")
                need(dve, "a_sig", l, 4)
                tmp = w_k
                step(STT(tmp, w_a, -1.0, over(col(l, "ka", 0, 4), T), ALU.add, ALU.mult))
                step(STT(c1024(k), c1024(tmp), 1.0, c1024(k), ALU.add, ALU.mult))
                for j in range(2):
                    b = bank(dve, ("kks", l, j))
                    up(TS(sq[:, 2 * j:2 * j + 2, :], b[:, :].rearrange("p (c t) -> p c t", c=2), 1e-24, None, ALU.max),
                       "kkmax")
                need(dve, "kkr", l, 1)
                step(V.reciprocal(c1024(sq), c1024(sq)))
                step(TTo(c1024(kk), c1024(kk), c1024(sq), ALU.mult))
                need(dve, "e2", l, 4)
                e1 = w_e1.rearrange("p c t s n -> p (c t) s n")
                ar = w_ar.rearrange("p c t s n -> p (c t) s n")
                ct = lambda ap: ap.rearrange("p c (t n) -> p (c t) n", t=TT)
                up(STT(ar[:, :, 0, :], ct(kk), -1.0, e1[:, :, 0, :], ALU.mult, ALU.mult), "ar")
                up(TTo(ar[:, :, 1, :], ct(w_xm[:, 0:4, :]), e1[:, :, 1, :], ALU.mult), "ar")
                step(TTo(c1024(w_b), c1024(kk), c1024(w_a), ALU.mult))
                up(TTo(c1024(w_k), c1024(k), c1024(w_e2), ALU.mult), "kb")
                up(TTo(c1024(w_b), c1024(w_b), c1024(w_e2), ALU.mult), "kb")
                step(TTo(c1024(sq), c1024(k), c1024(w_xm[:, 0:4, :]), ALU.mult))
                up(TTo(sq, sq, over(col(l, "rk", 0, 4), T), ALU.mult), "rk")
                up(V.reciprocal(rec4, w_e1[:, :, 1, 0, 0]), "dve_step")
                own(dve, "dve_step")
                up(TTo(sS, w_e1[:, :, 0, 1, P - 1], rec4, ALU.mult), "dve_step")
                v = w_xm[:, 8:12, :]
                if l == 0:
                    up(V.tensor_copy(vfirst, v), "v_fin")
                else:
                    need(dve, "vsig", 0, 4)
                    step(TTo(c1024(w_kk), c1024(vfirst), c1024(v), ALU.subtract))
                    step(TTo(c1024(w_kk), c1024(w_kk), c1024(w_a), ALU.mult))
                    up(TTo(c1024(v), c1024(v), c1024(w_kk), ALU.add), "v_fin")
                b = bank(dve, ("bon", l))
                up(V.tensor_copy(bons, b[:, 0:16]), "bon")
                own(dve, "bon")
                for tt in range(TT):
                    core(l, tt)

            def core(l, tt):
                for g in range(2):
                    for h in range(4 * g, 4 * g + 4):
                        b = bank(dve, ("A", l, tt, h))
                        up(TTo(w_AT[:, h].rearrange("p q n -> p (q n)"), b[:, :], cst("mask4"), ALU.mult), "AT")
                    own(dve, "AT")
                    hs = slice(4 * g, 4 * g + 4)
                    step(TTo(w_XT[:, hs, :], w_AT[:, hs, 0, :], rep(cst("merge", 0, 128), 4), ALU.mult))
                    up(TTo(w_XT[:, hs, :], w_XT[:, hs, :], rep(cst("ident"), 4), ALU.add), "XTi")
                    own(dve, "XTi")
                for v in range(LEVELS):
                    for g in range(2):
                        hs = slice(4 * g, 4 * g + 4)
                        if v < LEVELS - 1:
                            b = bank(dve, ("XU", l, tt, v, g))
                            if v == 0:
                                need(dve, "Xi", l, 2 * tt + g + 1)
                            up(TTo(w_X[:, hs, :], w_X[:, hs, :], b[:, :].rearrange("p (h n) -> p h n", h=4), ALU.add), "Xu")
                        b = bank(dve, ("XTU", l, tt, v, g))
                        up(TTo(w_XT[:, hs, :], w_XT[:, hs, :], b[:, :].rearrange("p (h n) -> p h n", h=4), ALU.add), "XTu")
                    own(dve, "XTu")
                    if v < LEVELS - 1:
                        own(dve, "Xu")
                if tt == 0:
                    need(dve, "S_zero", l, 1)
                    b = bank(dve, ("S", l))[:, :].rearrange("p (c n) -> p c n", c=CT)
                    for q in range(2):
                        s = slice(64 * q, 64 * q + 64)
                        up(TTo(w_S[s, :, s], b[s, :, s], over(sS[s, :], DH), ALU.mult), "Sbd")
                need(dve, "yraw", l, tt + 1)
                h8 = lambda ap: ap.rearrange("p (h n) -> p h n", h=8)
                step(V.tensor_reduce(m8[:, 0:8], h8(w_y), AX.X, ALU.add))
                step(TS(m8[:, 0:8], m8[:, 0:8], 1.0 / DH, None, ALU.mult))
                step(TTo(h8(w_y), h8(w_y), over(m8[:, 0:8], DH), ALU.subtract))
                step(TTo(w_t, w_y, w_y, ALU.mult))
                up(V.tensor_reduce(v8[:, 0:8], h8(w_t), AX.X, ALU.add), "rw_ss")
                own(dve, "rw_ss")
                step(TTo(h8(w_t), h8(w_vt[:, tt, :]), over(bons[:, 8 * tt:8 * tt + 8], DH), ALU.mult))
                need(dve, "rw_rstd", l, tt + 1)
                step(TTo(h8(w_y), h8(w_y), over(v8r[:, 0:8], DH), ALU.mult))
                step(TTo(w_y, w_y, row("gnw"), ALU.mult))
                step(TTo(w_y, w_y, row("gnb"), ALU.add))
                step(TTo(w_y, w_y, w_t, ALU.add))
                up(TTo(w_o[:, tt, :], w_y, w_g[:, tt, :], ALU.mult), "yrw")

            def merge(l):
                n = 0
                for i in range(3):
                    for half in range(2):
                        for tt in range(TT):
                            need(dve, "gsig", l, n + 1)
                            b = bank(dve, ("br", l, i, half, tt))
                            out = xn[:, tt, half * W:(half + 1) * W]
                            if n >= 4:
                                dve.wait_ge(sem("merged"), l * 12 + n - 1)
                            up(TTo(prod[:, n % 2, :], b[:, :], gates[:, n, :], ALU.mult), "brprod")
                            own(dve, "brprod")
                            if i:
                                ins = TTo(out, out, prod[:, n % 2, :], ALU.add)
                            else:
                                ins = V.tensor_copy(out, prod[:, n % 2, :])
                            up(ins, "merged")
                            n += 1
                for j in range(4):
                    b = bank(dve, ("mT", l, j))
                    up(V.tensor_copy(hT[:, 2 * j:2 * j + 2, :], b[:, :].rearrange("p (c t) -> p c t", c=2)), "mT")
                for half in range(2):
                    for tt in range(TT):
                        b = bank(dve, ("out", l, half, tt))
                        x = X[:, tt, half * W:(half + 1) * W]
                        up(TTo(x, x, b[:, :], ALU.add), "xmix")

            def dense():
                for n in range(D_FF // 256):
                    need(dve, "fsig", 0, n + 1)
                    s = f_s[:, n % 2, :]
                    up(TTo(s, s, bank(dve, ("fg", n))[:, :], ALU.mult), "fgt")
                    own(dve, "fgt")
                    b = bank(dve, ("fu", n))
                    up(TTo(f_h[:, 2 * n:2 * n + 2, :].rearrange("p f t -> p (f t)"), s, b[:, :], ALU.mult), "fhid")
                dve.wait_ge(sem("fdown"), PER["fdown"])
                for tt in range(TT):
                    for half in range(2):
                        x = X[:, tt, half * W:(half + 1) * W]
                        up(TTo(x, x, psum[4 + 2 * tt + half][:, :], ALU.add), "xffn")
                own(dve, "xffn")

            def route():
                up(V.tensor_copy(lg, bank(dve, ("route",))[:, 0:16]), "lg")
                own(dve, "lg")
                for tt in range(TT):
                    s = slice(8 * tt, 8 * tt + 8)
                    step(V.max(mx8[:, s], lg[:, s]))
                    step(V.max_index(idx8[:, s], mx8[:, s], lg[:, s]))
                    step(V.tensor_copy(idxf[:, s], idx8[:, s]))
                    step(TS(oh1[:, s], cst("iota8"), idxf[:, 8 * tt:8 * tt + 1], None, ALU.is_equal))
                    step(TS(oh2[:, s], cst("iota8"), idxf[:, 8 * tt + 1:8 * tt + 2], None, ALU.is_equal))
                    up(TTo(sel8[:, s], oh1[:, s], oh2[:, s], ALU.add), "sel")
                    up(TTo(ex[:, tt:tt + 1], mx8[:, 8 * tt + 1:8 * tt + 2], mx8[:, 8 * tt:8 * tt + 1], ALU.subtract), "top")
                    dve.wait_ge(sem("topexp"), tt + 1)
                    w1, w2 = w12[:, 2 * tt:2 * tt + 1], w12[:, 2 * tt + 1:2 * tt + 2]
                    step(TS(w1, ex[:, tt:tt + 1], 1.0, None, ALU.add))
                    step(V.reciprocal(w1, w1))
                    step(TTo(w2, w1, ex[:, tt:tt + 1], ALU.mult))
                    step(TS(oh1[:, s], oh1[:, s], w1, None, ALU.mult))
                    up(STT(gate8[:, s], oh2[:, s], w2, oh1[:, s], ALU.mult, ALU.add), "sel")
                b = bank(dve, ("rank",))
                up(V.tensor_copy(pos8, b[:, 0:16]), "rank")
                up(V.tensor_reduce(flagf[:, 0:1], b[:, 16:24], AX.X, ALU.max), "rank")
                own(dve, "rank")
                up(V.tensor_copy(flag[:, :], flagf[:, 0:1]), "e_flag")

            def experts(n0):
                if n0:
                    step(TS(pos8, pos8, -float(P), None, ALU.add))
                with dve.Fori(0, N_EXP) as e0:
                    e = e0 + n0
                    for i, src in enumerate((pos8, sel8, gate8)):
                        up(V.tensor_copy(cur[:, 2 * i:2 * i + 2], src.rearrange("p (t e) -> p t e", t=TT)
                                         [:, :, bass.ds(e0, 1)].rearrange("p t e -> p (t e)")), "e_cur")
                    dve.wait_ge(sem("e_cur"), 3 * e + 3)
                    for i, dst in ((1, e_P), (2, e_G)):
                        for tt in range(TT):
                            up(TS(dst[:, tt, :], cst("slot"), cur[:, tt:tt + 1], cur[:, 2 * i + tt:2 * i + tt + 1],
                                  ALU.is_equal, ALU.mult), "e_onehot")
                    for j in range(2):
                        dve.wait_ge(sem("e_gather"), 3 * e + j + 1)
                        up(TTo(e_x[:, 4 * j:4 * j + 4, :], psum[j][:, :].rearrange("p (k n) -> p k n", k=4),
                               over(col(DEPTH - 1, "norm2", 4 * j, 4), P), ALU.mult), "e_x")
                    for ch in range(FCH):
                        s = e_s[:, ch % 2, :]
                        dve.wait_ge(sem("e_sig"), 7 * e + ch + 1)
                        up(TTo(s, s, psum[2 * (ch % 2)][:, :], ALU.mult), "e_gated")
                        dve.wait_ge(sem("e_gated"), 7 * e + ch + 1)
                        dve.wait_ge(sem("e_up"), 14 * e + 2 * ch + 2)
                        up(TTo(e_h[:, ch % 2, :], s, psum[2 * (ch % 2) + 1][:, :], ALU.mult), "e_hid")
                    for tt in range(TT):
                        for half in range(2):
                            dve.wait_ge(sem("e_comb"), 4 * e + 2 * tt + half + 1)
                            x = X[:, tt, half * W:(half + 1) * W]
                            up(TTo(x, x, psum[2 * tt + half][:, :], ALU.add), "e_add")
                    dve.wait_ge(sem("e_add"), 4 * e + 4)

            dve.wait_ge(sem("const"), 16)
            dve.wait_ge(sem("pcol"), 16)
            x_ready(dve, 0)
            for l in range(DEPTH):
                norm(l, 2 * l, "norm1")
                ssm(l)
                retention(l)
                rwkv(l)
                merge(l)
                norm(l, 2 * l + 1, "norm2")
                if l == 0:
                    dense()
                else:
                    route()
            experts(0)
            overflow(dve, experts)
            up(V.tensor_copy(cur[:, 0:1], cur[:, 1:2]), "x_final")
            dve.wait_ge(sem("rstd_final"), 1)
            dve.wait_ge(sem("finw"), 16)
            for tt in range(TT):
                up(STT(xn[:, tt, :], X[:, tt, :], rs[:, tt:tt + 1], finw, ALU.mult, ALU.mult), "normed")

        @block.gpsimd
        def _(pool):
            G = nc.gpsimd

            def step(ins):
                up(ins, "pool_step")
                own(pool, "pool_step")

            def rsqrt(out, x, n, scale, eps, sig):
                step(G.tensor_scalar(out, x, scale, eps, ALU.mult, ALU.add))
                up(G.tensor_tensor(out, out, cst("neghalf").to_broadcast([P, n]), ALU.pow), sig)

            def norm(n):
                need(pool, "sumsq", n, 2)
                rsqrt(rs, ss, 2, 1.0 / D, RMS_EPS, "rstd")

            def ssm(l):
                if l:
                    need(pool, "xffn", 0, 4)
                up(G.memset(s_raw[:, :, 0:3], 0.0), "xbc_zero")
                need(pool, "dt_done", l, 2)
                up(G.tensor_copy(s_ab, over(a_tok, P)), "a_bcast")
                h8 = lambda ap: ap.rearrange("p (h n) -> p h n", h=8)
                for tt in range(TT):
                    need(pool, "xs_tok", l, tt + 1)
                    up(G.tensor_tensor(h8(s_xdt[:, tt, :]), h8(s_xs[:, tt, :]), over(dt_tok[:, 8 * tt:8 * tt + 8], DH),
                                       ALU.mult), "xdt")
                need(pool, "cs_exp", l, 1)
                own(pool, "xdt")
                up(G.tensor_tensor(h8(s_xdd), h8(s_xdt[:, 0, :]), over(ecs[:, 8:16], DH), ALU.mult), "xdd")
                for tt in range(TT):
                    up(G.tensor_tensor(h8(s_dx[:, tt, :]), h8(s_xs[:, tt, :]), over(row("dskip"), DH), ALU.mult), "dxs")
                for tt in range(TT):
                    need(pool, "ssm_ss", l, tt + 1)
                    rsqrt(g2r[:, 0:2], g2[:, 0:2], 2, 1.0 / 256, RMS_EPS, "ssm_rstd")

            def retention(l):
                need(pool, "yT", l, 8)
                up(G.memset(r_kv, 0.0), "kv_zero")
                for j in range(4):
                    need(pool, "qraw", l, j + 1)
                    s = slice(2 * j, 2 * j + 2)
                    up(G.tensor_tensor(r_qk[:, s, :], r_raw[:, s, :], rep(cst("cos"), 2), ALU.mult), "qcos")
                for tt in range(TT):
                    need(pool, "ret_ss", l, tt + 1)
                    rsqrt(r8r[:, 0:8], r8[:, 0:8], 8, 1.0 / DH, RMS_EPS, "ret_rstd")

            def rwkv(l):
                need(pool, "yT", l, 10)
                up(G.memset(w_raw[:, :, 0:1], 0.0), "raw_zero")
                up(G.memset(w_S, 0.0), "S_zero")
                for tt in range(TT):
                    for v in range(LEVELS):
                        for g in range(2):
                            if v == 0:
                                need(pool, "AT", l, 8 * tt + 4 * g + 4)
                            else:
                                bank(pool, ("P1", l, tt, v - 1, g))
                            hs = slice(4 * g, 4 * g + 4)
                            up(G.tensor_tensor(w_LT[:, hs, :], w_AT[:, hs, 0, :], rep(cst("merge", v + 1, 128), 4),
                                               ALU.mult), "LTm")
                    need(pool, "rw_ss", l, tt + 1)
                    rsqrt(v8r[:, 0:8], v8[:, 0:8], 8, 1.0 / DH, GN_EPS, "rw_rstd")

            pool.wait_ge(sem("const"), 16)
            for l in range(DEPTH):
                norm(2 * l)
                ssm(l)
                retention(l)
                rwkv(l)
                norm(2 * l + 1)
            pool.wait_ge(sem("sumsq"), 2 * (2 * DEPTH + 1))
            rsqrt(rs, ss, 2, 1.0 / D, RMS_EPS, "rstd_final")


def kernel(**inputs):
    import concourse.bacc as bacc
    from concourse.bass_utils import run_bass_kernel_spmd

    a = {k: np.ascontiguousarray(v) for k, v in inputs.items()}

    def tiles(v):
        v = np.asarray(v)
        return v.reshape(v.shape[0], -1, P).transpose(0, 2, 1)

    v0 = np.concatenate([np.zeros((DEPTH - len(a["rw_v0"]), W), np.float32), a["rw_v0"]], 0)
    cw = a["ssm_conv_w"].reshape(DEPTH, XBC_TILES, P, TAPS).transpose(0, 2, 1, 3).reshape(DEPTH, P, -1)
    pcol = np.concatenate([tiles(a["norm1_w"]), tiles(a["norm2_w"]), tiles(a["rw_mu"]), tiles(a["rw_k_k"]),
                           tiles(a["rw_k_a"]), tiles(a["rw_a0"]), tiles(a["rw_r_k"].reshape(DEPTH, -1)), tiles(v0),
                           tiles(a["ssm_norm_w"]), cw, tiles(a["ssm_conv_b"])], 2)
    prow = np.concatenate([a["rw_w0"], a["rw_gn_w"], a["rw_gn_b"], a["ssm_dt_bias"], a["ssm_a_log"], a["ssm_d"]], 1)
    feeds = dict(x=a["x"], const=constants(), pcol=np.ascontiguousarray(pcol), prow=np.ascontiguousarray(prow))
    for name in ("w_in", "rw_w_up", "rw_a_up", "rw_g_up", "rw_v_down", "rw_v_up", "w_branch", "w_out", "ffn_wg",
                 "ffn_wu", "ffn_wd", "moe_router", "moe_wg", "moe_wu", "moe_wd", "final_norm_w"):
        feeds[name] = a[name]
    nc = bacc.Bacc("TRN2", target_bir_lowering=False, num_devices=1)
    t = {k: nc.dram_tensor(f"in_{k}", v.shape, F32, kind="ExternalInput").ap() for k, v in feeds.items()}
    t["out"] = nc.dram_tensor("out", a["x"].shape, F32, kind="ExternalOutput").ap()
    trunk(nc, t)
    r = run_bass_kernel_spmd(nc, [{f"in_{k}": v for k, v in feeds.items()}], core_ids=[0])
    return r.results[0]["out"]
```

```python
from contextlib import ExitStack

import numpy as np

import concourse.bass as bass
from concourse import mybir

ALU = mybir.AluOpType
ACT = mybir.ActivationFunctionType
AX = mybir.AxisListType
F32 = mybir.dt.float32
F32R = mybir.dt.float32r
I32 = mybir.dt.int32
U32 = mybir.dt.uint32

P = 128
T = 256
TT = T // P
D = 1024
KT = D // P
W = 512
CT = W // P
HEADS, DH = 8, 64
DEPTH = 2
RW_COLS = 3 * W + 64 + 64 + 128
SSM_COLS = W + 1024 + 8
XBC_TILES = 8
TAPS = 4
D_FF, N_EXP, D_FFE = 2816, 8, 3584
FCH = D_FFE // W
RMS_EPS, GN_EPS = 1e-6, 64e-5
LEVELS = 6
SLOTS = 4
QUARTER = 1024
RING = 4
RAW = 7
LAG = 3
RW_ORDER = (12, 4, 6, 0, 2, 8, 10)



def quarters(chunks, last):
    def some(kind, ch):
        return [(kind, ch, q) for q in range(last if ch == chunks - 1 else 4)]

    out = []
    for ch in range(chunks):
        out += some("g", ch) + some("u", ch)
        if ch:
            out += some("d", ch - 1)
    return out + some("d", chunks - 1)


DENSE_CH = -(-D_FF // W)
DENSE_SEQ = quarters(DENSE_CH, 2)
MOE_SEQ = quarters(FCH, 4)
NQ = len(MOE_SEQ)


def first(seq, kind, ch):
    return min(i for i, x in enumerate(seq) if x[:2] == (kind, ch))


def last(seq, kind, ch):
    return max(i for i, x in enumerate(seq) if x[:2] == (kind, ch))


def moe_plan():
    pe, act, dve = ({i: [] for i in range(NQ)} for _ in range(3))
    for ch in range(FCH):
        g, u = last(MOE_SEQ, "g", ch), last(MOE_SEQ, "u", ch)
        act[g + LAG].append(("sigmoid", ch))
        dve[g + LAG].append(("gated", ch))
        dve[u + LAG].append(("hidden", ch))
        turn = first(MOE_SEQ, "g", ch + 1) + 5 if ch < FCH - 1 else first(MOE_SEQ, "d", FCH - 2) + 3
        pe[turn].append(("turn", ch))
        act[turn + LAG - 1].append(("high", ch))
        dve[turn + LAG - 1].append(("low", ch))
    act[LAG - 1].append(("rows", 0))
    pe[5].append(("combine", 0))
    pe[7].append(("combine", 1))
    dve[7].append(("add", 0))
    dve[9].append(("add", 1))
    at = first(MOE_SEQ, "g", FCH - 1) + 1
    dve[at - 8].append(("onehot", 0))
    pe[at].append(("gather", 0))
    dve[at + 2].append(("scaled", 0))
    act[at + 3].append(("xhigh", 0))
    dve[at + 4].append(("xlow", 0))
    pe[at + 7].append(("gates", 0))
    act[at + 9].append(("gates", 0))
    return pe, act, dve


CONSTS = [("ident", 128), ("neghalf", 1), ("ucent", 256), ("mask4", 512), ("merge", 128 * 7), ("rest", 128),
          ("ones", 128), ("headones", 128), ("swap", 128), ("cos", 256), ("sin", 256),
          ("decay", 1024), ("zeta", 8), ("xi", 8), ("headsel", 2), ("iota8", 8), ("slot", 128)]
FIRST_CONSTS = 129
COLS = [("norm1", 8), ("norm2", 8), ("mu", 14), ("kk", 4), ("ka", 4), ("a0", 4), ("rk", 4),
        ("v0", 4), ("ssmn", 4), ("convw", 32), ("convb", 8)]
ROWS = [("w0", 512), ("gnw", 512), ("gnb", 512), ("dtb", 8), ("alog", 8), ("dskip", 8)]


def offsets(table):
    at, out = 0, {}
    for name, n in table:
        out[name] = (at, n)
        at += n
    return out, at


CONST_AT, CONST_N = offsets(CONSTS)
COL_AT, COL_N = offsets(COLS)
ROW_AT, ROW_N = offsets(ROWS)


def constants():
    f = np.float32
    s, t = np.arange(P)[:, None], np.arange(P)[None, :]
    incl, strict = (s <= t), (s < t)
    mid = (s <= P // 2 - 1)
    rate = np.exp(-0.5)
    c = {}
    c["ucent"] = -rate * np.concatenate([strict.astype(np.float64) - mid, incl.astype(np.float64) - mid], 1)
    c["mask4"] = np.concatenate([strict, incl, strict, incl], 1)
    c["ident"] = np.eye(P)
    merge = []
    for b in (1, 2, 4, 8, 16, 32, 64):
        merge.append((s // (2 * b) == t // (2 * b)) & (s % (2 * b) < b) & (t % (2 * b) >= b))
    c["merge"] = np.concatenate(merge, 1)
    c["rest"] = (s > t)
    c["ones"] = np.ones((P, P))
    c["headones"] = (s // DH == t // DH)
    c["swap"] = (s == (t ^ 1))
    half = DH // 2
    inv = (np.float32(10000.0) ** (-np.arange(half, dtype=f) / f(half))).astype(f)
    ang = np.arange(T, dtype=f)[None, :] * inv[(np.arange(P) % DH) // 2][:, None]
    c["cos"] = np.cos(ang)
    c["sin"] = np.sin(ang) * np.where(np.arange(P) % 2 == 0, -1.0, 1.0)[:, None]
    lg = np.log1p(-np.exp2(-5.0 - np.arange(HEADS)))
    order = [0, 2, 4, 6, 1, 3, 5, 7]
    dec = [np.where(incl, np.exp(np.where(incl, t - s, 0) * lg[h]), 0.0) * DH ** -0.5 for h in order]
    c["decay"] = np.concatenate(dec, 1)
    c["zeta"] = np.exp((P - 1 - s) * lg[None, :]) * DH ** -0.5
    c["xi"] = np.exp((s + 1.0) * lg[None, :])
    c["headsel"] = (s // DH == np.arange(2)[None, :])
    c["iota8"] = np.broadcast_to(np.arange(8), (P, 8))
    c["slot"] = np.broadcast_to(np.arange(P), (P, P))
    c["neghalf"] = np.full((P, 1), -0.5)
    return np.ascontiguousarray(np.concatenate([np.asarray(c[n], f) for n, _ in CONSTS], 1))


PER = dict(sumsq=2, rstd=2, xn=2, hT=4,
           dt_raw=1, dt_na=1, dt_exp=1, dt_u=1, dt_ln=1, a_exp=1, dt_done=2, a_bcast=1, cs_sb=1, cs_exp=1,
           seg=16, segexp=4, gmat=4, cbm=2, xbc_raw=4, xbc_zero=1, conv=8, convsig=8, xbcT=8,
           xs_tok=2, b_tok=1, xdt=2, xdd=1, dxs=2, st_sb=1, yd_used=2, yo_used=1, zsig=2, zsilu=2,
           ssm_ss=2, ssm_rstd=2, yssm=2, yT=12,
           qraw=4, qcos=4, rot_used=4, qkT=4, rv=2, rgsig=2, rgate=2, scT=4, kz=1, kv_zero=1, kvbd=2,
           ry_used=2, rc_used=1, ret_ss=2, ret_rstd=2, yret=2,
           rw_raw=7, raw_zero=1, xm=14, xw_tanh=1, xg_sig=1, lwz=2, lw=2, gtok=2, a_sig=4, e1=4, e2=4,
           kksq=1, kkmax=2, kkr=1, rk=1, ar=2, kb=2, v_fin=1, vtok=2, bon=1, kb_tok=2,
           AT=16, XTi=4, Xi=4, LTm=24, P1=24, Xu=20, XTu=24, w_tok=2, u_tok=2, S_zero=1, Sbd=2,
           yraw=2, rw_ss=2, rw_rstd=2, yrw=2,
           gsig=12, brprod=12, merged=12, mT=4, xmix=4,
           vd=1, vsig=4, hTh=4, hTl=4, fgt=11, fhid=11, fsig=11, fhh=11, fhl=11, xffn=4, q_hi=0, q_lo=0, q_used=0, lg=1, sel=4, rank=2)
SHARED = dict(softplus=("dt_raw", "dt_na", "dt_u", "dt_done"), decays=("a_exp", "dt_exp", "dt_ln"),
              ssm_tok=("xs_tok", "b_tok", "st_sb"), scaled_x=("xdt", "xdd", "dxs"),
              zeroed=("xbc_zero", "kv_zero", "raw_zero", "S_zero"), squares=("ssm_ss", "ret_ss", "rw_ss"),
              rsqrts=("ssm_rstd", "ret_rstd", "rw_rstd"), y_done=("yssm", "yret", "yrw"),
              loras=("xw_tanh", "xg_sig"), sigmoids=("zsig", "rgsig"), silus=("zsilu", "rgate"))
SHARE = {name: (group, sum(PER[x] for x in names[:i]), sum(PER[x] for x in names))
         for group, names in SHARED.items() for i, name in enumerate(names)}
PARAMS = (5 * 16, 12 * 16)


def trunk(nc, t):
    ctx = ExitStack()
    with ctx:
        def sb(name, cols, dt=F32):
            return ctx.enter_context(nc.sbuf_tensor(name, [P, cols], dt))

        sems = {}

        def sem(name):
            name = SHARE[name][0] if name in SHARE else name
            if name not in sems:
                sems[name] = ctx.enter_context(nc.semaphore("s_" + name))
            return sems[name]

        counts = {}

        def up(ins, name):
            group = SHARE[name][0] if name in SHARE else name
            counts[group] = counts.get(group, 0) + 1
            return ins.then_inc(sem(name), 1)

        def need(eng, name, l, k):
            _, before, per = SHARE.get(name, (name, 0, PER[name]))
            eng.wait_ge(sem(name), l * per + before + k)

        def own(eng, name):
            eng.wait_ge(sem(name), counts[SHARE[name][0] if name in SHARE else name])

        X = sb("X", TT * D)[:, :].rearrange("p (t d) -> p t d", t=TT)
        xn = sb("xn", TT * D)[:, :].rearrange("p (t d) -> p t d", t=TT)
        hT = sb("hT", KT * T)[:, :].rearrange("p (k t) -> p k t", k=KT)
        slab = sb("slab", SLOTS * KT * W)[:, :].rearrange("p (s n) -> p s n", s=SLOTS)
        const = sb("const", CONST_N)
        pcol = sb("pcol", DEPTH * COL_N)
        prow = sb("prow", ROW_N)
        wa_up = sb("wa_up", W)
        g_up = sb("g_up", W)
        v_down = sb("v_down", CT * 32)[:, :].rearrange("p (c n) -> p c n", c=CT)
        v_up = sb("v_up", W)
        wdt = sb("wdt", KT * 8)[:, :].rearrange("p (k n) -> p k n", k=KT)
        router = sb("router", KT * 8)[:, :].rearrange("p (k n) -> p k n", k=KT)
        small = sb("small", 660)
        yT = sb("yT", 3 * CT * T)[:, :].rearrange("p (b c t) -> p b c t", b=3, c=CT)
        finw = yT[:, 0].rearrange("p c t -> p (c t)")
        vfirst = sb("vfirst", CT * T)[:, :].rearrange("p (c t) -> p c t", c=CT)
        KB = 256
        with nc.sbuf_tensor("arena", [P, 70 * KB], F32) as arena:
            pass
        split = ctx.enter_context(nc.sbuf_tensor("split", [P, 64 * KB], F32R))
        arena_end = sb("arena_end", 6 * KB)
        psum = [ctx.enter_context(nc.psum_tensor(f"bank{b}", [P, 512], F32)) for b in range(8)]

        def area(kb, cols):
            a = int(kb * KB)
            assert a + cols <= 70 * KB, (kb, cols)
            return arena[:, a:a + cols]

        def cst(name, i=0, n=None):
            a, m = CONST_AT[name]
            n = m if n is None else n
            return const[:, a + i * n:a + i * n + n]

        def col(l, name, i, n=1):
            a = l * COL_N + COL_AT[name][0] + i
            return pcol[:, a:a + n]

        def row(name):
            a, n = ROW_AT[name]
            return prow[:, a:a + n]

        def over(ap, n):
            return ap.unsqueeze(2).to_broadcast([ap.shape[0], ap.shape[1], n])

        def rep(ap, n):
            return ap.unsqueeze(1).to_broadcast([ap.shape[0], n, ap.shape[1]])

        small_at = [0]

        def sm(n):
            a = small_at[0]
            small_at[0] += n
            assert small_at[0] <= 660
            return small[:, a:a + n]

        ss, rs = sm(2), sm(2)
        dtr, dtm, dna, dte, dtu, dln = sm(16), sm(16), sm(16), sm(16), sm(16), sm(16)
        dd, dz, dq = sm(16), sm(16), sm(16)
        dt_tok, a_tok, a_neg, cs, ecs = sm(16), sm(16), sm(8), sm(24), sm(16)
        g2, g2r = sm(4), sm(4)
        r8, r8r = sm(16), sm(16)
        m8, v8, v8r = sm(16), sm(16), sm(16)
        bons, rec4, sS = sm(16), sm(4), sm(4)
        lg, mx8, idxf, oh1, oh2 = sm(16), sm(16), sm(16), sm(16), sm(16)
        ex, w12, flagf = sm(2), sm(4), sm(8)
        gate9, sel9, pos9 = (sm(2 * (N_EXP + 1)).rearrange("p (t e) -> p t e", t=TT) for _ in range(3))
        cur = sm(8)
        idx8 = sb("idx8", 16, U32)
        flag = sb("flag", 1, I32)

        s_raw = area(0, 8 * 259).rearrange("p (c t) -> p c t", c=8)
        s_xbc = area(8.25, 2048).rearrange("p (c t) -> p c t", c=8)
        s_acc = area(16.25, 2048).rearrange("p (c t) -> p c t", c=8)
        s_sig = area(24.25, 2048).rearrange("p (c t) -> p c t", c=8)
        s_xs = area(32.25, 1024).rearrange("p (t n) -> p t n", t=TT)
        s_xdt = area(36.25, 1024).rearrange("p (t n) -> p t n", t=TT)
        s_xdd = area(40.25, 512)
        s_bt = area(42.25, 256)
        s_ab = area(43.25, 2048).rearrange("p (h n) -> p h n", h=16)
        s_L = area(51.25, 1024).rearrange("p (b h n) -> p b h n", b=2, h=4)
        s_G = area(55.25, 2048).rearrange("p (t h n) -> p t h n", t=TT, h=8)
        s_z = area(63.25, 1024).rearrange("p (t n) -> p t n", t=TT)
        s_st = area(67.25, 512)
        s_cb = area(0, 512).rearrange("p (t g n) -> p t g n", t=TT, g=2)
        s_y = area(24.25, 1024).rearrange("p (t n) -> p t n", t=TT)
        s_sq = area(28.25, 512)
        s_dx = area(2.25, 1024).rearrange("p (t n) -> p t n", t=TT)
        r_raw = area(0, 2048).rearrange("p (c t) -> p c t", c=8)
        r_qk = area(8, 2048).rearrange("p (c t) -> p c t", c=8)
        r_t = area(16, 512).rearrange("p (c t) -> p c t", c=2)
        r_v = area(18, 1024).rearrange("p (t n) -> p t n", t=TT)
        r_g = area(22, 1024).rearrange("p (t n) -> p t n", t=TT)
        r_sc = area(26, 2048).rearrange("p (t q i n) -> p t q i n", t=TT, q=2, i=4)
        r_kz = area(34, 512)
        r_kv = area(36, 512).rearrange("p (c n) -> p c n", c=CT)
        r_y = area(38, 1024).rearrange("p (t n) -> p t n", t=TT)
        r_sq = area(42, 512)
        w_raw = area(0, 14 * 257).rearrange("p (c t) -> p c t", c=14)
        w_ar = area(0, 2048).rearrange("p (c t s n) -> p c t s n", c=CT, t=TT, s=2)
        w_k = area(8, 1024).rearrange("p (c t) -> p c t", c=CT)
        w_b = area(12, 1024).rearrange("p (c t) -> p c t", c=CT)
        w_xm = area(16, 14 * 256).rearrange("p (c t) -> p c t", c=14)
        w_e1 = area(30, 2048).rearrange("p (c t s n) -> p c t s n", c=CT, t=TT, s=2)
        w_e2 = area(38, 1024).rearrange("p (c t) -> p c t", c=CT)
        w_a = area(42, 1024).rearrange("p (c t) -> p c t", c=CT)
        w_kk = area(46, 1024).rearrange("p (c t) -> p c t", c=CT)
        w_sq = area(50, 1024).rearrange("p (c t) -> p c t", c=CT)
        w_lw = area(54, 1024).rearrange("p (t n) -> p t n", t=TT)
        w_g = area(58, 1024).rearrange("p (t n) -> p t n", t=TT)
        w_vt = area(62, 1024).rearrange("p (t n) -> p t n", t=TT)
        w_S = area(66, 512).rearrange("p (c n) -> p c n", c=CT)
        w_vd = area(68, 256)
        w_AT = area(16, 4096).rearrange("p (h q n) -> p h q n", h=8, q=4)
        w_LT = area(32, 1024).rearrange("p (h n) -> p h n", h=8)
        w_X = area(36, 1024).rearrange("p (h n) -> p h n", h=8)
        w_XT = area(40, 1024).rearrange("p (h n) -> p h n", h=8)
        w_P1 = area(44, 1024).rearrange("p (h n) -> p h n", h=8)
        w_kt = area(48, 512)
        w_bt = area(50, 512)
        w_w = area(52, 512)
        w_u = area(54, 512)
        w_y = xn[:, 0, 0:512]
        w_t = xn[:, 0, 512:1024]
        w_o = xn[:, 1, :].rearrange("p (t n) -> p t n", t=TT)
        gates = area(0, 12 * 512).rearrange("p (i n) -> p i n", i=12)
        prod = area(24, 1024).rearrange("p (b n) -> p b n", b=2)
        def ring(i):
            a = 2 * QUARTER * (i % RING)
            return split[:, a:a + QUARTER], split[:, a + QUARTER:a + 2 * QUARTER]

        at = 2 * QUARTER * RING
        hTh = split[:, at:at + 2048].rearrange("p (k t) -> p k t", k=KT)
        hTl = split[:, at + 2048:at + 4096].rearrange("p (k t) -> p k t", k=KT)
        f_hh = split[:, at + 4096:at + 6144].rearrange("p (b f t) -> p b f t", b=2, f=4)
        f_hl = split[:, at + 6144:at + 8192].rearrange("p (b f t) -> p b f t", b=2, f=4)
        f_s = xn[:, 0, :].rearrange("p (j n) -> p j n", j=2)
        e_xh = split[:, at:at + 2048].rearrange("p (b k n) -> p b k n", b=2, k=KT)
        e_xl = split[:, at + 2048:at + 4096].rearrange("p (b k n) -> p b k n", b=2, k=KT)
        e_hh = split[:, at + 4096:at + 5120].rearrange("p (b f n) -> p b f n", b=2, f=4)
        e_hl = split[:, at + 5120:at + 6144].rearrange("p (b f n) -> p b f n", b=2, f=4)
        flat = hT.rearrange("p k t -> p (k t)")
        e_xf = flat[:, 0:1024].rearrange("p (k n) -> p k n", k=KT)
        e_P = flat[:, 1024:1280].rearrange("p (t n) -> p t n", t=TT)
        e_G = flat[:, 1280:1536].rearrange("p (t n) -> p t n", t=TT)
        e_GT = flat[:, 1536:2048].rearrange("p (b n) -> p b n", b=2)
        half_slab = KT * W // 2
        whole = slab.rearrange("p s n -> p (s n)")
        e_raw = [whole[:, i * half_slab:(i + 1) * half_slab] for i in range(RAW)]
        spare = whole[:, RAW * half_slab:(RAW + 1) * half_slab]
        e_s = spare[:, 0:1024].rearrange("p (b n) -> p b n", b=2)
        e_h = spare[:, 1024:2048].rearrange("p (b n) -> p b n", b=2)
        e_y = arena_end[:, 0:1024]

        def plain(ap):
            return ap.bitcast(F32)

        where, turn, left = {}, {"G": 0, "A": 0}, {}
        base = {"G": 0, "A": 4}
        filled = [0] * 8

        def open_bank(pe, pool, name, sig, l, k):
            b = base[pool] + turn[pool] % 4
            turn[pool] += 1
            if b in left:
                need(pe, *left[b])
            left[b] = (sig, l, k)
            filled[b] += 1
            where[name] = (b, filled[b])
            return psum[b]

        def full(mm, name):
            mm.then_inc(sem(f"full{where[name][0]}"), 1)

        def bank(eng, name):
            b, n = where[name]
            eng.wait_ge(sem(f"full{b}"), n)
            return psum[b]

        slabs, spent_by = [], {}

        def use_slab(pe, key):
            n = len(slabs)
            slabs.append(key)
            pe.wait_ge(sem(f"slab{n % SLOTS}"), 16 * (n // SLOTS + 1))
            return slab[:, n % SLOTS, :]

        def x_ready(eng, n, tt):
            if n == 0:
                eng.wait_ge(sem("xin"), 16)
            elif n % 2:
                need(eng, "xmix", n // 2, 2 * tt + 2)
            else:
                need(eng, "xffn", 0, 2 * tt + 2)

        def overflow(eng, experts):
            eng.wait_ge(sem("e_flag"), 1)
            most = eng.value_load(flag[0:1, 0:1], min_val=0, max_val=T)
            with eng.If(most > P):
                experts(1)

        block = ctx.enter_context(nc.Block())

        @block.tensor
        def _(pe):
            mm, tr = nc.tensor.matmul, nc.tensor.transpose
            ident = cst("ident")

            def spent(n, name):
                spent_by[n] = (f"full{where[name][0]}", where[name][1])

            def norm(n):
                banks = [open_bank(pe, "G", ("xT", n, j), "hT", n, j + 1) for j in range(4)]
                for tt in range(TT):
                    need(pe, "xn", n, tt + 1)
                    for j, b in enumerate(banks):
                        for i in range(2):
                            m = tr(b[:, i * T + tt * P:i * T + tt * P + P],
                                   xn[:, tt, (2 * j + i) * P:(2 * j + i + 1) * P], ident)
                        if tt == TT - 1:
                            full(m, ("xT", n, j))
                need(pe, "hT", n, 4)

            def channel_pair(b, w, c0):
                for i in range(2):
                    for k in range(KT):
                        m = mm(b[:, i * T:(i + 1) * T], w[:, k, c0 + i * P:c0 + (i + 1) * P], hT[:, k, :],
                               start=k == 0, stop=k == KT - 1)
                return m

            def token_tile(b, w, tt):
                for k in range(KT):
                    m = mm(b[:, :], hT[:, k, tt * P:(tt + 1) * P], w[:, k, :], start=k == 0, stop=k == KT - 1)
                return m

            def view(s, cols=W):
                return s[:, 0:KT * cols].rearrange("p (k n) -> p k n", k=KT)

            def pairs(l, key, jobs):
                w = view(use_slab(pe, key), 256 if len(jobs) == 1 else W)
                for n, (name, sig, k) in enumerate(jobs):
                    b = open_bank(pe, "G", name, sig, l, k)
                    full(channel_pair(b, w, 2 * P * n), name)
                spent(len(slabs) - 1, name)

            def tiles(l, key, names, sig, k0):
                w = view(use_slab(pe, key))
                for tt in range(TT):
                    b = open_bank(pe, "G", names[tt], sig, l, k0 + tt + 1)
                    full(token_tile(b, w, tt), names[tt])
                spent(len(slabs) - 1, names[-1])

            def turn_y(l, i, src, sig, k):
                per = 4 if i == 1 else 1
                k0 = {1: 0, 2: 8, 0: 10}[i]
                for tt in range(TT):
                    need(pe, sig, l, tt + 1)
                    b = open_bank(pe, "A", ("yT", l, i, tt), "yT", l, k0 + per * (tt + 1))
                    for c in range(CT):
                        m = tr(b[:, c * P:(c + 1) * P], src[:, tt, c * P:(c + 1) * P], ident)
                    full(m, ("yT", l, i, tt))

            def conv_in(l, s):
                pairs(l, ("xbc", l, s), [(("xbc", l, 2 * s + j), "xbc_raw", 2 * s + j + 1) for j in range(2)])

            def ssm(l):
                pe.wait_ge(sem("params"), PARAMS[l])
                b = open_bank(pe, "G", ("dt", l), "dt_raw", l, 1)
                for tt in range(TT):
                    for k in range(KT):
                        m = mm(b[:, 8 * tt:8 * tt + 8], hT[:, k, tt * P:(tt + 1) * P], wdt[:, k, :],
                               start=k == 0, stop=k == KT - 1)
                full(m, ("dt", l))
                conv_in(l, 0)
                need(pe, "dt_done", l, 2)
                pe.wait_ge(sem("const"), 16)
                b = open_bank(pe, "A", ("cs", l), "cs_sb", l, 1)
                for i, (mask, tt) in enumerate((("incl", 0), ("incl", 1), ("rest", 0))):
                    lhs = cst("rest") if mask == "rest" else cst("mask4", 1, 128)
                    m = mm(b[:, 8 * i:8 * i + 8], lhs, a_tok[:, 8 * tt:8 * tt + 8], start=True, stop=True)
                full(m, ("cs", l))
                conv_in(l, 1)
                need(pe, "a_bcast", l, 1)
                for tt in range(TT):
                    for g in range(2):
                        b = open_bank(pe, "A", ("seg", l, tt, g), "seg", l, 4 * (2 * tt + g + 1))
                        for h in range(4):
                            m = mm(b[:, h * P:(h + 1) * P], s_ab[:, 8 * tt + 4 * g + h, :], cst("mask4", 1, 128),
                                   start=True, stop=True)
                        full(m, ("seg", l, tt, g))
                tiles(l, ("z", l), [("z", l, tt) for tt in range(TT)], "zsilu", 0)
                query_keys(l, 0)
                need(pe, "xbcT", l, 8)
                for tt in range(TT):
                    b = open_bank(pe, "A", ("cb", l, tt), "cbm", l, tt + 1)
                    for g in range(2):
                        m = mm(b[:, g * P:(g + 1) * P], s_xbc[:, 4 + g, tt * P:(tt + 1) * P],
                               s_xbc[:, 6 + g, tt * P:(tt + 1) * P], start=True, stop=True)
                    full(m, ("cb", l, tt))
                for tt in range(TT):
                    b = open_bank(pe, "A", ("xst", l, tt), "xs_tok", l, tt + 1)
                    for c in range(CT):
                        m = tr(b[:, c * P:(c + 1) * P], s_xbc[:, c, tt * P:(tt + 1) * P], ident)
                    full(m, ("xst", l, tt))
                b = open_bank(pe, "A", ("bt", l), "b_tok", l, 1)
                for g in range(2):
                    m = tr(b[:, g * P:(g + 1) * P], s_xbc[:, 4 + g, 0:P], ident)
                full(m, ("bt", l))
                query_keys(l, 1)
                need(pe, "xdd", l, 1)
                need(pe, "b_tok", l, 1)
                b = open_bank(pe, "A", ("st", l), "st_sb", l, 1)
                for g in range(2):
                    m = mm(b[:, g * T:(g + 1) * T], s_bt[:, g * P:(g + 1) * P], s_xdd[:, g * T:(g + 1) * T],
                           start=True, stop=True)
                full(m, ("st", l))
                query_keys(l, 2)
                for tt in range(TT):
                    need(pe, "gmat", l, 2 * tt + 2)
                    need(pe, "xdt", l, tt + 1)
                    b = open_bank(pe, "A", ("yd", l, tt), "yd_used", l, tt + 1)
                    for h in range(HEADS):
                        m = mm(b[:, h * DH:(h + 1) * DH], s_G[:, tt, h, :], s_xdt[:, tt, h * DH:(h + 1) * DH],
                               start=True, stop=True)
                    full(m, ("yd", l, tt))
                need(pe, "st_sb", l, 1)
                b = open_bank(pe, "A", ("yo", l), "yo_used", l, 1)
                for g in range(2):
                    m = mm(b[:, g * T:(g + 1) * T], s_xbc[:, 6 + g, P:T], s_st[:, g * T:(g + 1) * T],
                           start=True, stop=True)
                full(m, ("yo", l))
                query_keys(l, 3)
                turn_y(l, 1, s_y, "yssm", 0)

            half_used = [None]

            def query_keys(l, n):
                if n % 2 == 0:
                    half_used[0] = view(use_slab(pe, ("rqk", l, n // 2)))
                b = open_bank(pe, "G", ("qk", l, n), "qraw", l, n + 1)
                full(channel_pair(b, half_used[0], 2 * P * (n % 2)), ("qk", l, n))
                if n % 2:
                    spent(len(slabs) - 1, ("qk", l, n))

            def retention(l):
                for j in range(4):
                    need(pe, "qraw", l, j + 1)
                    b = open_bank(pe, "A", ("rot", l, j), "rot_used", l, j + 1)
                    full(mm(b[:, :], cst("swap"), r_raw[:, 2 * j:2 * j + 2, :], start=True, stop=True), ("rot", l, j))
                tiles(l, ("rv", l), [("rv", l, tt) for tt in range(TT)], "rv", 0)
                tiles(l, ("rg", l), [("rg", l, tt) for tt in range(TT)], "rgate", 0)
                need(pe, "qkT", l, 4)
                for tt in range(TT):
                    for q in range(2):
                        b = open_bank(pe, "A", ("sc", l, tt, q), "scT", l, 2 * tt + q + 1)
                        for i in range(4):
                            m = mm(b[:, i * P:(i + 1) * P], r_qk[64 * q:64 * q + 64, 4 + i, tt * P:(tt + 1) * P],
                                   r_qk[64 * q:64 * q + 64, i, tt * P:(tt + 1) * P], start=True, stop=True)
                        full(m, ("sc", l, tt, q))
                b = open_bank(pe, "A", ("kt", l), "kz", l, 1)
                for c in range(CT):
                    m = tr(b[:, c * P:(c + 1) * P], r_qk[:, 4 + c, 0:P], ident)
                full(m, ("kt", l))
                need(pe, "kz", l, 1)
                need(pe, "rv", l, 2)
                b = open_bank(pe, "A", ("kv", l), "kvbd", l, 2)
                for c in range(CT):
                    m = mm(b[:, c * P:(c + 1) * P], r_kz[:, c * P:(c + 1) * P], r_v[:, 0, c * P:(c + 1) * P],
                           start=True, stop=True)
                full(m, ("kv", l))
                for tt in range(TT):
                    need(pe, "scT", l, 2 * tt + 2)
                    b = open_bank(pe, "A", ("ry", l, tt), "ry_used", l, tt + 1)
                    for h in range(HEADS):
                        m = mm(b[:, h * DH:(h + 1) * DH], r_sc[:, tt, h % 2, h // 2, :],
                               r_v[:, tt, h * DH:(h + 1) * DH], start=True, stop=True)
                    full(m, ("ry", l, tt))
                pairs(l, ("lora", l), [(("rw", l, 0), "rw_raw", 1)])
                need(pe, "kvbd", l, 2)
                b = open_bank(pe, "A", ("rc", l), "rc_used", l, 1)
                for c in range(CT):
                    m = mm(b[:, c * P:(c + 1) * P], r_qk[:, c, P:T], r_kv[:, c, :], start=True, stop=True)
                full(m, ("rc", l))
                rwkv_in(l, 0)
                turn_y(l, 2, r_y, "yret", 0)

            def rwkv_in(l, s):
                pairs(l, (("rwk", "rwr", "rwv")[s], l),
                      [(("rw", l, 1 + 2 * s + j), "rw_raw", 2 + 2 * s + j) for j in range(2)])

            def gate(l, i, half, tt):
                if tt == 0:
                    half_used[0] = view(use_slab(pe, ("gate", l, i, half)))
                n = 4 * i + 2 * half + tt
                b = open_bank(pe, "G", ("gate", l, i, half, tt), "gsig", l, n + 1)
                full(token_tile(b, half_used[0], tt), ("gate", l, i, half, tt))
                if tt == TT - 1:
                    spent(len(slabs) - 1, ("gate", l, i, half, tt))

            def rwkv(l):
                for s in (1, 2):
                    rwkv_in(l, s)
                need(pe, "xw_tanh", l, 1)
                for tt in range(TT):
                    b = open_bank(pe, "A", ("lw", l, tt), "lwz", l, tt + 1)
                    full(mm(b[:, :], w_xm[0:64, 12, tt * P:(tt + 1) * P], wa_up[0:64, :], start=True, stop=True),
                         ("lw", l, tt))
                for j in range(2):
                    b = open_bank(pe, "A", ("a", l, j), "a_sig", l, 2 * j + 2)
                    for i in range(2):
                        c = 2 * j + i
                        m = mm(b[:, i * T:(i + 1) * T], wa_up[64:128, c * P:(c + 1) * P], w_xm[64:128, 12, :],
                               start=True, stop=True)
                    full(m, ("a", l, j))
                need(pe, "xg_sig", l, 1)
                for tt in range(TT):
                    b = open_bank(pe, "A", ("g", l, tt), "gtok", l, tt + 1)
                    full(mm(b[:, :], w_xm[:, 13, tt * P:(tt + 1) * P], g_up[:, :], start=True, stop=True), ("g", l, tt))
                need(pe, "lw", l, 2)
                for c in range(CT):
                    b = open_bank(pe, "A", ("cum", l, c), "e2", l, c + 1)
                    for tt in range(TT):
                        m = mm(b[:, tt * T:(tt + 1) * T], w_lw[:, tt, c * P:(c + 1) * P], cst("ucent"),
                               start=True, stop=True)
                    full(m, ("cum", l, c))
                need(pe, "kksq", l, 1)
                for j in range(2):
                    b = open_bank(pe, "A", ("kks", l, j), "kkmax", l, j + 1)
                    full(mm(b[:, :], cst("headones"), w_sq[:, 2 * j:2 * j + 2, :], start=True, stop=True),
                         ("kks", l, j))
                gate(l, 0, 0, 0)
                if l > 0:
                    need(pe, "xm", l, 14)
                    b = open_bank(pe, "A", ("vd", l), "vd", 0, 1)
                    for c in range(CT):
                        m = mm(b[0:32, 0:T], v_down[:, c, :], w_xm[:, 8 + c, :], start=c == 0, stop=c == CT - 1)
                    full(m, ("vd", l))
                    need(pe, "vd", 0, 1)
                    for j in range(2):
                        b = open_bank(pe, "A", ("vu", l, j), "vsig", 0, 2 * j + 2)
                        for i in range(2):
                            c = 2 * j + i
                            m = mm(b[:, i * T:(i + 1) * T], v_up[0:32, c * P:(c + 1) * P], w_vd[0:32, :],
                                   start=True, stop=True)
                        full(m, ("vu", l, j))
                gate(l, 0, 0, 1)
                need(pe, "ar", l, 2)
                need(pe, "kb", l, 2)
                core(l, 0)
                core(l, 1)
                gate(l, 0, 1, 1)
                turn_y(l, 0, w_o, "yrw", 0)

            def rows(l):
                need(pe, "v_fin", l, 1)
                for tt in range(TT):
                    b = open_bank(pe, "A", ("vT", l, tt), "vtok", l, tt + 1)
                    for c in range(CT):
                        m = tr(b[:, c * P:(c + 1) * P], w_xm[:, 8 + c, tt * P:(tt + 1) * P], ident)
                    full(m, ("vT", l, tt))
                need(pe, "rk", l, 1)
                b = open_bank(pe, "A", ("bon", l), "bon", l, 1)
                for tt in range(TT):
                    for c in range(CT):
                        m = mm(b[:, 8 * tt + 2 * c:8 * tt + 2 * c + 2], w_sq[:, c, tt * P:(tt + 1) * P], cst("headsel"),
                               start=True, stop=True)
                full(m, ("bon", l))
                for i, src in enumerate((w_k, w_b)):
                    b = open_bank(pe, "A", ("kbt", l, i), "kb_tok", l, i + 1)
                    for c in range(CT):
                        m = tr(b[:, c * P:(c + 1) * P], src[:, c, 0:P], ident)
                    full(m, ("kbt", l, i))

            def core(l, tt):
                for h in range(HEADS):
                    c, p0 = h // 2, 64 * (h % 2)
                    b = open_bank(pe, "A", ("A", l, tt, h), "AT", l, 8 * tt + h + 1)
                    rhs = w_ar[p0:p0 + 64, c, tt, :, :]
                    mm(b[:, 0:256], w_b[p0:p0 + 64, c, tt * P:(tt + 1) * P], rhs, start=True, stop=True)
                    full(mm(b[:, 256:512], w_k[p0:p0 + 64, c, tt * P:(tt + 1) * P], rhs, start=True, stop=True),
                         ("A", l, tt, h))
                    if tt == 0 and h == 3:
                        rows(l)
                for g in range(2):
                    need(pe, "XTi", l, 2 * tt + g + 1)
                    b = open_bank(pe, "A", ("X0", l, tt, g), "Xi", l, 2 * tt + g + 1)
                    for i in range(4):
                        m = tr(b[:, i * P:(i + 1) * P], w_XT[:, 4 * g + i, :], ident)
                    full(m, ("X0", l, tt, g))
                for v in range(LEVELS):
                    for g in range(2):
                        need(pe, "LTm", l, 12 * tt + 2 * v + g + 1)
                        if v == 0:
                            need(pe, "Xi", l, 2 * tt + g + 1)
                        else:
                            need(pe, "Xu", l, 10 * tt + 2 * (v - 1) + g + 1)
                        b = open_bank(pe, "A", ("P1", l, tt, v, g), "P1", l, 12 * tt + 2 * v + g + 1)
                        for i in range(4):
                            m = mm(b[:, i * P:(i + 1) * P], w_LT[:, 4 * g + i, :], w_X[:, 4 * g + i, :],
                                   start=True, stop=True)
                        full(m, ("P1", l, tt, v, g))
                    for g in range(2):
                        need(pe, "P1", l, 12 * tt + 2 * v + g + 1)
                        if v > 0:
                            need(pe, "XTu", l, 12 * tt + 2 * (v - 1) + g + 1)
                        if v < LEVELS - 1:
                            b = open_bank(pe, "A", ("XU", l, tt, v, g), "Xu", l, 10 * tt + 2 * v + g + 1)
                            for i in range(4):
                                m = mm(b[:, i * P:(i + 1) * P], w_XT[:, 4 * g + i, :], w_P1[:, 4 * g + i, :],
                                       start=True, stop=True)
                            full(m, ("XU", l, tt, v, g))
                        b = open_bank(pe, "A", ("XTU", l, tt, v, g), "XTu", l, 12 * tt + 2 * v + g + 1)
                        for i in range(4):
                            m = mm(b[:, i * P:(i + 1) * P], w_P1[:, 4 * g + i, :], w_XT[:, 4 * g + i, :],
                                   start=True, stop=True)
                        full(m, ("XTU", l, tt, v, g))
                need(pe, "vtok", l, 2)

                def heads_product(name, sig, terms, state):
                    b = open_bank(pe, "A", (name, l, tt), sig, l, tt + 1)
                    for c in range(CT):
                        if tt:
                            mm(b[:, c * P:(c + 1) * P], w_ar[:, c, tt, state, :], w_S[:, c, :], start=True, stop=False,
                               skip_group_check=True)
                        for h in (2 * c, 2 * c + 1):
                            for i, (lhs, rhs) in enumerate(terms):
                                m = mm(b[:, h * DH:(h + 1) * DH], lhs(h), rhs(h), start=(tt == 0 and i == 0),
                                       stop=i == len(terms) - 1, skip_group_check=True)
                    full(m, (name, l, tt))

                if tt:
                    need(pe, "Sbd", l, 2)
                heads_product("w", "w_tok", [(lambda h: w_AT[:, h, 2, :], lambda h: w_vt[:, tt, h * DH:(h + 1) * DH])], 0)
                need(pe, "w_tok", l, tt + 1)
                need(pe, "XTu", l, 12 * tt + 12)
                b = open_bank(pe, "A", ("u", l, tt), "u_tok", l, tt + 1)
                for h in range(HEADS):
                    m = mm(b[:, h * DH:(h + 1) * DH], w_XT[:, h, :], w_w[:, h * DH:(h + 1) * DH], start=True, stop=True)
                full(m, ("u", l, tt))
                if tt == 0:
                    gate(l, 0, 1, 0)
                need(pe, "u_tok", l, tt + 1)
                heads_product("y", "yraw", [(lambda h: w_AT[:, h, 3, :], lambda h: w_vt[:, tt, h * DH:(h + 1) * DH]),
                                            (lambda h: w_AT[:, h, 1, :], lambda h: w_u[:, h * DH:(h + 1) * DH])], 1)
                if tt == 0:
                    need(pe, "kb_tok", l, 2)
                    b = open_bank(pe, "A", ("S", l), "Sbd", l, 2)
                    for c in range(CT):
                        s = slice(c * P, (c + 1) * P)
                        mm(b[:, s], w_kt[:, s], w_vt[:, 0, s], start=True, stop=False)
                        m = mm(b[:, s], w_bt[:, s], w_u[:, s], start=False, stop=True)
                    full(m, ("S", l))

            def merge(l):
                for i in (1, 2):
                    for half in range(2):
                        for tt in range(TT):
                            gate(l, i, half, tt)
                n = 0
                for i in range(3):
                    w = use_slab(pe, ("branch", l, i)).rearrange("p (c n) -> p c n", c=CT)
                    need(pe, "yT", l, 12)
                    for half in range(2):
                        for tt in range(TT):
                            n += 1
                            b = open_bank(pe, "A", ("br", l, i, half, tt), "brprod", l, n)
                            for c in range(CT):
                                m = mm(b[:, :], yT[:, i, c, tt * P:(tt + 1) * P], w[:, c, half * W:(half + 1) * W],
                                       start=c == 0, stop=c == CT - 1)
                            full(m, ("br", l, i, half, tt))
                    spent(len(slabs) - 1, ("br", l, i, 1, 1))
                need(pe, "merged", l, 12)
                for j in range(4):
                    b = open_bank(pe, "G", ("mT", l, j), "mT", l, j + 1)
                    for i in range(2):
                        for tt in range(TT):
                            m = tr(b[:, i * T + tt * P:i * T + tt * P + P],
                                   xn[:, tt, (2 * j + i) * P:(2 * j + i + 1) * P], ident)
                    full(m, ("mT", l, j))
                need(pe, "mT", l, 4)
                ws = [view(use_slab(pe, ("out", l, half))) for half in range(2)]
                for tt in range(TT):
                    for half in range(2):
                        b = open_bank(pe, "G", ("out", l, half, tt), "xmix", l, 2 * tt + half + 1)
                        full(token_tile(b, ws[half], tt), ("out", l, half, tt))
                        if tt:
                            spent(len(slabs) - 2 + half, ("out", l, half, tt))

            def dense():
                for b in range(8):
                    if b in left:
                        need(pe, *left[b])
                    left[b] = ("xffn", 0, 4)
                need(pe, "hTl", 0, 4)
                for n, (kind, ch, q) in enumerate(DENSE_SEQ):
                    if q == 0:
                        use_slab(pe, ("f" + kind, ch))
                    hi, lo = ring(n)
                    nq = 4 if ch < DENSE_CH - 1 else 2
                    if kind != "d":
                        cols = W * nq // 4
                        per = QUARTER // cols
                        b0 = 0 if kind == "g" else 2
                        if q == 0 and ch:
                            need(pe, "fgt" if kind == "g" else "fhid", 0, 2 * ch)
                        need(pe, "q_lo", 0, n + 1)
                        for k in range(per):
                            kt = q * per + k
                            for c in range(cols // P):
                                out = psum[b0 + c // 2][:, (c % 2) * T:(c % 2 + 1) * T]
                                a = slice(k * cols + c * P, k * cols + (c + 1) * P)
                                mm(out, hi[:, a], hTh[:, kt, :], start=kt == 0 and c % 2 == 0, stop=False,
                                   skip_group_check=True)
                                mm(out, hi[:, a], hTl[:, kt, :], start=False, stop=False, skip_group_check=True)
                                m = mm(out, lo[:, a], hTh[:, kt, :], start=False, stop=kt == KT - 1,
                                       skip_group_check=True)
                    else:
                        if q == 0:
                            need(pe, "fhl", 0, 2 * ch + nq // 2)
                        need(pe, "q_lo", 0, n + 1)
                        for tt in range(TT):
                            for half in range(2):
                                out, ws = psum[4 + 2 * tt + half], slice(half * W, (half + 1) * W)
                                hs = slice(tt * P, (tt + 1) * P)
                                begin, end = ch == 0 and q == 0, ch == DENSE_CH - 1 and q == nq - 1
                                mm(out[:, :], f_hh[:, ch % 2, q, hs], hi[:, ws], start=begin, stop=False)
                                mm(out[:, :], f_hl[:, ch % 2, q, hs], hi[:, ws], start=False, stop=False)
                                m = mm(out[:, :], f_hh[:, ch % 2, q, hs], lo[:, ws], start=False, stop=end)
                    up(m, "q_used")
                    if q == nq - 1:
                        spent_by[len(slabs) - 1] = ("q_lo", n + 1)

            def route():
                b = open_bank(pe, "G", ("route",), "lg", 0, 1)
                pe.wait_ge(sem("router"), 16)
                for tt in range(TT):
                    for k in range(KT):
                        m = mm(b[:, 8 * tt:8 * tt + 8], hT[:, k, tt * P:(tt + 1) * P], router[:, k, :],
                               start=k == 0, stop=k == KT - 1)
                full(m, ("route",))
                need(pe, "sel", 0, 4)
                strict = cst("mask4", 0, 128)
                sel = [sel9[:, tt, 0:N_EXP] for tt in range(TT)]
                b = open_bank(pe, "G", ("rank",), "rank", 0, 2)
                mm(b[:, 0:8], strict, sel[0], start=True, stop=True)
                mm(b[:, 8:16], cst("ones"), sel[0], start=True, stop=False)
                mm(b[:, 8:16], strict, sel[1], start=False, stop=True)
                mm(b[:, 16:24], cst("ones"), sel[0], start=True, stop=False)
                full(mm(b[:, 16:24], cst("ones"), sel[1], start=False, stop=True), ("rank",))

            def gather(g, par):
                pe.wait_ge(sem("m_onehot"), 4 * g + 4)
                for j in range(2):
                    for i in range(4):
                        for tt in range(TT):
                            m = mm(psum[6 + j][:, i * P:(i + 1) * P], xn[:, tt, (4 * j + i) * P:(4 * j + i + 1) * P],
                                   e_P[:, tt, :], start=tt == 0, stop=tt == TT - 1)
                    up(m, "m_gather")

            def gates_of(g, par):
                pe.wait_ge(sem("m_xf"), 2 * g + 2)
                for tt in range(TT):
                    m = tr(psum[6][:, tt * P:(tt + 1) * P], e_G[:, tt, :], ident)
                up(m, "m_gather")

            def combine(p, e, par, tt):
                pe.wait_ge(sem("m_y"), 2 * p + 2 * e + 2)
                if tt:
                    pe.wait_ge(sem("m_add"), 4 * p + 4 * e + 2)
                for half in range(2):
                    up(mm(psum[6 + half][:, :], e_GT[:, par, tt * P:(tt + 1) * P], e_y[:, half * W:(half + 1) * W],
                          start=True, stop=True), "m_comb")

            def experts(p):
                pe.wait_ge(sem("m_zero"), 2 * p + 2)
                gather(9 * p, 0)
                gates_of(9 * p, 0)
                plan = moe_plan()[0]
                with pe.Fori(0, N_EXP // 2) as pair:
                    for par in range(2):
                        e = 2 * pair + (par + N_EXP * p)
                        for i, (kind, ch, q) in enumerate(MOE_SEQ):
                            for what, a in plan[i]:
                                if what == "turn":
                                    pe.wait_ge(sem("m_hid"), 7 * e + a + 1)
                                    if a == 0:
                                        pe.wait_ge(sem("m_add"), 4 * p + 4 * e + 4)
                                    if a == FCH - 1:
                                        pe.wait_ge(sem("m_gt"), e + p + 2)
                                    for f in range(4):
                                        m = tr(psum[6 + a % 2][:, f * P:(f + 1) * P],
                                               e_h[:, a % 2, f * P:(f + 1) * P], ident)
                                    up(m, "m_turn")
                                elif what == "combine":
                                    combine(p, e, 1 - par, a)
                                elif what == "gather":
                                    gather(e + p + 1, 1 - par)
                                else:
                                    gates_of(e + p + 1, 1 - par)
                            hi, lo = ring(i)
                            if q == 0 and kind == "g" and ch == 0:
                                pe.wait_ge(sem("m_xl"), 2 * (e + p) + 2)
                            if q == 0 and kind == "g" and ch >= 2:
                                pe.wait_ge(sem("m_hid"), 7 * e + ch - 1)
                            if q == 0 and kind == "d":
                                pe.wait_ge(sem("m_hl"), 7 * e + ch + 1)
                            pe.wait_ge(sem("m_lo"), NQ * e + i + 1)
                            if kind == "d":
                                for half in range(2):
                                    out, ws = psum[4 + half], slice(half * W, (half + 1) * W)
                                    begin, end = ch == 0 and q == 0, ch == FCH - 1 and q == 3
                                    mm(out[:, :], e_hh[:, ch % 2, q, :], hi[:, ws], start=begin, stop=False)
                                    mm(out[:, :], e_hl[:, ch % 2, q, :], hi[:, ws], start=False, stop=False)
                                    m = mm(out[:, :], e_hh[:, ch % 2, q, :], lo[:, ws], start=False, stop=end)
                            else:
                                out = psum[2 * (ch % 2) + (kind == "u")]
                                for k in range(2):
                                    kt, ws = 2 * q + k, slice(k * W, (k + 1) * W)
                                    mm(out[:, :], e_xh[:, par, kt, :], hi[:, ws], start=kt == 0, stop=False)
                                    mm(out[:, :], e_xl[:, par, kt, :], hi[:, ws], start=False, stop=False)
                                    m = mm(out[:, :], e_xh[:, par, kt, :], lo[:, ws], start=False, stop=kt == KT - 1)
                            up(m, "m_used")
                e = N_EXP * (p + 1)
                for tt in range(TT):
                    combine(p, e, 1, tt)
                pe.wait_ge(sem("m_add"), 4 * p + 4 * e + 4)

            pe.wait_ge(sem("const_first"), 16)
            for l in range(DEPTH):
                norm(2 * l)
                ssm(l)
                retention(l)
                rwkv(l)
                merge(l)
                norm(2 * l + 1)
                if l == 0:
                    dense()
                else:
                    route()
            need(pe, "rank", 0, 2)
            for _ in range(RING):
                up(pe.nop(), "m_used")
            experts(0)
            overflow(pe, experts)

        DENSE_SLAB0 = slabs.index(("fg", 0))

        @block.sync
        def _(sp):
            w_in = t["w_in"]
            rwc, ssc = 0, RW_COLS
            ret = RW_COLS + SSM_COLS
            gat = ret + 4 * W

            def src(key):
                k, l = key[0], key[1]
                if k in ("lora", "rwk", "rwr", "rwv", "xbc", "z", "rqk", "rv", "rg", "gate"):
                    c0 = {"lora": 3 * W, "rwk": W, "rwr": 0, "rwv": 2 * W, "z": ssc,
                          "rv": ret + 2 * W, "rg": ret + 3 * W}.get(k)
                    if k == "xbc":
                        c0 = ssc + W + key[2] * W
                    if k == "rqk":
                        c0 = ret + key[2] * W
                    if k == "gate":
                        c0 = gat + (2 * key[2] + key[3]) * W
                    n = 256 if k == "lora" else W
                    return w_in[l, :, c0:c0 + n].rearrange("(k p) n -> p k n", p=P), KT, n
                if k == "branch":
                    return t["w_branch"][l, key[2]].rearrange("(c p) n -> p c n", p=P), CT, D
                if k == "out":
                    return t["w_out"][l, :, key[2] * W:(key[2] + 1) * W].rearrange("(k p) n -> p k n", p=P), KT, W
                ch = key[1]
                if k in ("fg", "fu"):
                    n = min(W, D_FF - ch * W)
                    w = t["ffn_wg" if k == "fg" else "ffn_wu"]
                    return w[0, :, ch * W:ch * W + n].rearrange("(k p) n -> p k n", p=P), KT, n
                nf = min(4, 22 - 4 * ch)
                return t["ffn_wd"][0, ch * W:ch * W + nf * P, :].rearrange("(f p) n -> p f n", p=P), nf, D

            sp.dma_start(X, t["x"][0].rearrange("(t p) d -> p t d", p=P)).then_inc(sem("xin"), 16)
            sp.dma_start(const[:, 0:FIRST_CONSTS], t["const"][:, 0:FIRST_CONSTS])\
                .then_inc(sem("const_first"), 16)
            sp.dma_start(pcol[:, :].rearrange("p (l n) -> p l n", l=DEPTH), t["pcol"].rearrange("l p n -> p l n"))\
                .then_inc(sem("pcol"), 16)
            for n, key in enumerate(slabs):
                if n == 1:
                    sp.dma_start(const[:, FIRST_CONSTS:], t["const"][:, FIRST_CONSTS:]).then_inc(sem("const"), 16)
                if n >= SLOTS:
                    name, value = spent_by[n - SLOTS]
                    sp.wait_ge(sem(name), value)
                s, k, c = src(key)
                sp.dma_start(slab[:, n % SLOTS, 0:k * c].rearrange("p (k n) -> p k n", k=k), s)\
                    .then_inc(sem(f"slab{n % SLOTS}"), 16)

            def half_slab_in(e0, ahead, h, wait):
                kind, ch, q = MOE_SEQ[2 * h]
                for name, value in wait:
                    sp.wait_ge(sem(name), value)
                s = t[{"g": "moe_wg", "u": "moe_wu", "d": "moe_wd"}[kind]][0, ahead:]
                if kind == "d":
                    s = s[bass.ds(e0, 1), ch * W + q * P:ch * W + (q + 2) * P, :]
                else:
                    s = s[bass.ds(e0, 1), q * 2 * P:(q + 2) * 2 * P, ch * W:(ch + 1) * W]
                s = s.rearrange("e (k p) n -> p (e k) n", p=P)
                sp.dma_start(e_raw[h % RAW].rearrange("p (k n) -> p k n", k=2 if kind == "d" else 4), s)\
                    .then_inc(sem(f"raw{h % RAW}"), 16)

            halves = NQ // 2

            def experts(p):
                for h in range(RAW):
                    if p:
                        wait = [("m_lo", NQ * N_EXP * p - 2 * (RAW - h - 1))]
                    else:
                        wait = [spent_by[max(n for n in spent_by if n % SLOTS == h // 2)]]
                    half_slab_in(0, 0, h, wait)

                def rest(e0, more):
                    e = e0 + N_EXP * p
                    for h in range(RAW, halves):
                        ahead = MOE_SEQ[2 * h + 2:2 * h + 3] == [("d", 0, 0)]
                        wait = [("m_lo", NQ * e + (2 * (h - RAW + ahead) + 2))]
                        half_slab_in(e0, 0, h, [] if MOE_SEQ[2 * h] == ("d", 0, 0) else wait)
                    for h in range(RAW if more else 0):
                        half_slab_in(e0, 1, h, [("m_lo", NQ * e + (2 * (halves - RAW + h) + 2))])

                with sp.Fori(0, N_EXP - 1) as e0:
                    rest(e0, True)
                rest(N_EXP - 1, False)

            experts(0)
            overflow(sp, experts)
            sp.wait_ge(sem("normed"), 2)
            sp.dma_start(t["out"][0].rearrange("(t p) d -> p t d", p=P), xn).then_inc(sem("stored"), 16)
            sp.wait_ge(sem("stored"), 16)

        @block.scalar
        def _(act):
            A, copy, mul = nc.scalar.activation, nc.scalar.copy, nc.scalar.mul

            def params(l):
                if l:
                    need(act, "brprod", l - 1, PER["brprod"])
                for dst, s in ((prow[:, :], t["prow"][l:l + 1, :].partition_broadcast(P)),
                               (wa_up[0:64, :], t["rw_w_up"][l]), (wa_up[64:128, :], t["rw_a_up"][l]),
                               (g_up[:, :], t["rw_g_up"][l]),
                               (wdt, t["w_in"][l, :, RW_COLS + SSM_COLS - 8:RW_COLS + SSM_COLS]
                                .rearrange("(k p) n -> p k n", p=P))):
                    act.dma_start(dst, s).then_inc(sem("params"), 16)
                if l:
                    act.dma_start(v_down, t["rw_v_down"][l - 1].rearrange("(c p) n -> p c n", p=P))\
                        .then_inc(sem("params"), 16)
                    act.dma_start(v_up[0:32, :], t["rw_v_up"][l - 1]).then_inc(sem("params"), 16)

            def norm(n):
                for tt in range(TT):
                    x_ready(act, n, tt)
                    up(A(xn[:, tt, :], X[:, tt, :], ACT.Square, accum_out=ss[:, tt:tt + 1]), "sumsq")
                for tt in range(TT):
                    need(act, "rstd", n, tt + 1)
                    up(mul(xn[:, tt, :], X[:, tt, :], rs[:, tt:tt + 1]), "xn")

            def turn_y(l, i):
                for tt in range(TT):
                    b = bank(act, ("yT", l, i, tt))
                    if i == 1:
                        for c in range(CT):
                            up(mul(yT[:, i, c, tt * P:(tt + 1) * P], b[:, c * P:(c + 1) * P], col(l, "ssmn", c)), "yT")
                    else:
                        up(copy(yT[:, i, :, tt * P:(tt + 1) * P], b[:, :].rearrange("p (c n) -> p c n", c=CT)), "yT")

            def ssm(l):
                act.wait_ge(sem("params"), PARAMS[l])
                up(A(a_neg, row("alog"), ACT.Exp), "a_exp")
                need(act, "dt_na", l, 1)
                up(A(dte, dna, ACT.Exp), "dt_exp")
                need(act, "dt_u", l, 1)
                up(A(dln, dtu, ACT.Ln), "dt_ln")
                need(act, "xbc_zero", l, 1)
                for j in range(4):
                    b = bank(act, ("xbc", l, j))
                    up(copy(s_raw[:, 2 * j:2 * j + 2, 3:3 + T], b[:, :].rearrange("p (c t) -> p c t", c=2)), "xbc_raw")
                for c in range(XBC_TILES):
                    need(act, "conv", l, c + 1)
                    up(A(s_sig[:, c, :], s_acc[:, c, :], ACT.Sigmoid, bias=col(l, "convb", c)), "convsig")
                for tt in range(TT):
                    b = bank(act, ("z", l, tt))
                    up(A(s_z[:, tt, :], b[:, :], ACT.Sigmoid), "zsig")
                need(act, "cs_sb", l, 1)
                up(A(ecs, cs[:, 8:24], ACT.Exp), "cs_exp")

                def decay(q):
                    need(act, "seg", l, 4 * q + 4)
                    up(A(s_L[:, q % 2], s_L[:, q % 2], ACT.Exp), "segexp")

                decay(0)
                decay(1)
                for tt in range(TT):
                    b = bank(act, ("xst", l, tt))
                    up(copy(s_xs[:, tt, :], b[:, :]), "xs_tok")
                b = bank(act, ("bt", l))
                up(copy(s_bt, b[:, 0:T]), "b_tok")
                decay(2)
                decay(3)
                b = bank(act, ("st", l))
                up(copy(s_st, b[:, :]), "st_sb")
                turn_y(l, 1)

            def retention(l):
                for j in range(4):
                    b = bank(act, ("qk", l, j))
                    up(copy(r_raw[:, 2 * j:2 * j + 2, :], b[:, :].rearrange("p (c t) -> p c t", c=2)), "qraw")
                for tt in range(TT):
                    b = bank(act, ("rv", l, tt))
                    up(copy(r_v[:, tt, :], b[:, :]), "rv")
                for tt in range(TT):
                    b = bank(act, ("rg", l, tt))
                    up(A(r_g[:, tt, :], b[:, :], ACT.Sigmoid), "rgsig")
                need(act, "kv_zero", l, 1)
                b = bank(act, ("kv", l))[:, :].rearrange("p (c n) -> p c n", c=CT)
                for q in range(2):
                    s = slice(64 * q, 64 * q + 64)
                    up(copy(r_kv[s, :, s], b[s, :, s]), "kvbd")
                turn_y(l, 2)

            def rwkv(l):
                need(act, "raw_zero", l, 1)
                for j in range(7):
                    b = bank(act, ("rw", l, j))
                    c = RW_ORDER[j]
                    up(copy(w_raw[:, c:c + 2, 1:1 + T], b[:, :].rearrange("p (c t) -> p c t", c=2)), "rw_raw")
                    if j == 2:
                        need(act, "xm", l, 2)
                        up(A(w_xm[0:64, 12, :], w_xm[0:64, 12, :], ACT.Tanh), "xw_tanh")
                        up(A(w_xm[:, 13, :], w_xm[:, 13, :], ACT.Sigmoid), "xg_sig")
                for tt in range(TT):
                    need(act, "lwz", l, tt + 1)
                    up(A(w_lw[:, tt, :], w_lw[:, tt, :], ACT.Sigmoid), "lw")
                for j in range(2):
                    b = bank(act, ("a", l, j))
                    for i in range(2):
                        c = 2 * j + i
                        up(A(w_a[:, c, :], b[:, i * T:(i + 1) * T], ACT.Sigmoid, bias=col(l, "a0", c)), "a_sig")
                for tt in range(TT):
                    b = bank(act, ("g", l, tt))
                    up(copy(w_g[:, tt, :], b[:, :]), "gtok")
                for c in range(CT):
                    b = bank(act, ("cum", l, c))
                    up(A(w_e1[:, c], b[:, :].rearrange("p (t s n) -> p t s n", t=TT, s=2), ACT.Exp), "e1")
                    up(A(w_e2[:, c, :].rearrange("p (t n) -> p t n", t=TT),
                         b[:, :].rearrange("p (t s n) -> p t s n", t=TT, s=2)[:, :, 1, :], ACT.Exp, scale=-1.0), "e2")
                need(act, "kkmax", l, 2)
                up(A(w_sq, w_sq, ACT.Sqrt), "kkr")
                if l > 0:
                    b = bank(act, ("vd", l))
                    up(copy(w_vd[0:32, :], b[0:32, 0:T]), "vd")
                    need(act, "kb", l, 2)
                    for j in range(2):
                        b = bank(act, ("vu", l, j))
                        for i in range(2):
                            c = 2 * j + i
                            up(A(w_a[:, c, :], b[:, i * T:(i + 1) * T], ACT.Sigmoid, bias=col(l, "v0", c)), "vsig")
                for tt in range(TT):
                    b = bank(act, ("vT", l, tt))
                    up(copy(w_vt[:, tt, :], b[:, :]), "vtok")
                for i, dst in enumerate((w_kt, w_bt)):
                    b = bank(act, ("kbt", l, i))
                    up(copy(dst, b[:, :]), "kb_tok")
                for tt in range(TT):
                    for g in range(2):
                        b = bank(act, ("X0", l, tt, g))
                        up(copy(w_X[:, 4 * g:4 * g + 4, :], b[:, :].rearrange("p (h n) -> p h n", h=4)), "Xi")
                    for v in range(LEVELS):
                        for g in range(2):
                            b = bank(act, ("P1", l, tt, v, g))
                            up(copy(w_P1[:, 4 * g:4 * g + 4, :], b[:, :].rearrange("p (h n) -> p h n", h=4)), "P1")
                    b = bank(act, ("w", l, tt))
                    up(copy(w_w, b[:, :]), "w_tok")
                    b = bank(act, ("u", l, tt))
                    up(copy(w_u, b[:, :]), "u_tok")
                    b = bank(act, ("y", l, tt))
                    if tt:
                        need(act, "yrw", l, tt)
                    up(copy(w_y, b[:, :]), "yraw")
                turn_y(l, 0)

            def merge(l):
                n = 0
                for i in range(3):
                    for half in range(2):
                        for tt in range(TT):
                            b = bank(act, ("gate", l, i, half, tt))
                            up(A(gates[:, n, :], b[:, :], ACT.Sigmoid), "gsig")
                            n += 1

            def split_high():
                for j in range(4):
                    need(act, "hT", 1, j + 1)
                    up(copy(hTh[:, 2 * j:2 * j + 2, :], hT[:, 2 * j:2 * j + 2, :]), "hTh")

            def dense():
                tasks = {}
                for ch in range(DENSE_CH):
                    g, u = last(DENSE_SEQ, "g", ch), last(DENSE_SEQ, "u", ch)
                    tasks.setdefault(min(g + LAG, len(DENSE_SEQ) - 1), []).append(("sigmoid", ch, g))
                    tasks.setdefault(min(u + LAG + 1, len(DENSE_SEQ) - 1), []).append(("high", ch, u))
                n_slab = DENSE_SLAB0 - 1
                for n, (kind, ch, q) in enumerate(DENSE_SEQ):
                    if q == 0:
                        n_slab += 1
                        act.wait_ge(sem(f"slab{n_slab % SLOTS}"), 16 * (n_slab // SLOTS + 1))
                    if n >= RING:
                        need(act, "q_used", 0, n - RING + 1)
                    up(copy(ring(n)[0], slab[:, n_slab % SLOTS, q * QUARTER:(q + 1) * QUARTER]), "q_hi")
                    for what, c, at_q in tasks.get(n, []):
                        for j in range(2 if c < DENSE_CH - 1 else 1):
                            if what == "sigmoid":
                                if c:
                                    need(act, "fhl", 0, 2 * c)
                                need(act, "q_used", 0, at_q + 1)
                                up(A(f_s[:, j, :], psum[j][:, :], ACT.Sigmoid), "fsig")
                            else:
                                need(act, "fhid", 0, 2 * c + j + 1)
                                up(copy(f_hh[:, c % 2, 2 * j:2 * j + 2, :].rearrange("p f t -> p (f t)"), f_s[:, j, :]),
                                   "fhh")

            def experts(p):
                def task(what, a, e, par):
                    if what == "sigmoid":
                        act.wait_ge(sem("m_used"), RING + NQ * e + last(MOE_SEQ, "g", a) + 1)
                        up(A(e_s[:, a % 2, :], psum[2 * (a % 2)][:, :], ACT.Sigmoid), "m_sig")
                    elif what == "high":
                        act.wait_ge(sem("m_turn"), 7 * e + a + 1)
                        up(copy(e_hh[:, a % 2], psum[6 + a % 2][:, :].rearrange("p (f n) -> p f n", f=4)), "m_hh")
                    elif what == "rows":
                        for half in range(2):
                            act.wait_ge(sem("m_used"), RING + NQ * e)
                            up(copy(e_y[:, half * W:(half + 1) * W], psum[4 + half][:, :]), "m_y")
                    elif what == "xhigh":
                        xhigh(e + p + 1, 1 - par)
                    else:
                        gates_of(e + p + 1, 1 - par)

                def xhigh(g, par):
                    for j in range(2):
                        act.wait_ge(sem("m_xf"), 2 * g + j + 1)
                        up(copy(e_xh[:, par, 4 * j:4 * j + 4, :], e_xf[:, 4 * j:4 * j + 4, :]), "m_xh")

                def gates_of(g, par):
                    act.wait_ge(sem("m_gather"), 3 * g + 3)
                    up(copy(e_GT[:, par, :], psum[6][:, 0:T]), "m_gt")

                xhigh(9 * p, 0)
                gates_of(9 * p, 0)
                plan = moe_plan()[1]
                with act.Fori(0, N_EXP // 2) as pair:
                    for par in range(2):
                        e = 2 * pair + (par + N_EXP * p)
                        for i in range(NQ):
                            h = i // 2
                            if i % 2 == 0:
                                act.wait_ge(sem(f"raw{h % RAW}"), 16 * ((NQ // 2 // RAW) * e + h // RAW + 1))
                            act.wait_ge(sem("m_used"), NQ * e + i + 1)
                            up(copy(ring(i)[0], e_raw[h % RAW][:, (i % 2) * QUARTER:(i % 2 + 1) * QUARTER]), "m_hi")
                            for what, a in plan[i]:
                                task(what, a, e, par)
                task("rows", 0, N_EXP * (p + 1), 0)

            for l in range(DEPTH):
                params(l)
                norm(2 * l)
                if l == 0:
                    act.wait_ge(sem("pcol"), 16)
                    act.dma_start(router, t["moe_router"][0].rearrange("(k p) n -> p k n", p=P))\
                        .then_inc(sem("router"), 16)
                ssm(l)
                retention(l)
                rwkv(l)
                merge(l)
                norm(2 * l + 1)
                if l == 0:
                    split_high()
                    dense()
            need(act, "brprod", DEPTH - 1, PER["brprod"])
            act.dma_start(finw, t["final_norm_w"].rearrange("(a d) -> a d", a=1).partition_broadcast(P))\
                .then_inc(sem("finw"), 16)
            for tt in range(TT):
                act.wait_ge(sem("top"), tt + 1)
                up(A(ex[:, tt:tt + 1], ex[:, tt:tt + 1], ACT.Exp), "topexp")
            experts(0)
            overflow(act, experts)
            act.wait_ge(sem("x_final"), 1)
            for tt in range(TT):
                up(A(xn[:, tt, :], X[:, tt, :], ACT.Square, accum_out=ss[:, tt:tt + 1]), "sumsq")

        @block.vector
        def _(dve):
            V = nc.vector
            TTo, TS, STT = V.tensor_tensor, V.tensor_scalar, V.scalar_tensor_tensor

            def step(ins):
                up(ins, "dve_step")
                own(dve, "dve_step")

            def norm(l, n, w):
                for j in range(4):
                    b = bank(dve, ("xT", n, j))
                    up(TTo(hT[:, 2 * j:2 * j + 2, :], b[:, :].rearrange("p (c t) -> p c t", c=2),
                           over(col(l, w, 2 * j, 2), T), ALU.mult), "hT")

            def ssm(l):
                dve.wait_ge(sem("params"), PARAMS[l])
                b = bank(dve, ("dt", l))
                up(TTo(dtr.rearrange("p (t h) -> p t h", t=TT), b[:, 0:16].rearrange("p (t h) -> p t h", t=TT),
                       rep(row("dtb"), TT), ALU.add), "dt_raw")
                own(dve, "dt_raw")
                up(STT(dna, dtr, -1.0, dtr, ALU.mult, ALU.min), "dt_na")
                up(TS(dtm, dtr, 0.0, None, ALU.max), "dve_step")
                need(dve, "dt_exp", l, 1)
                up(TS(dtu, dte, 1.0, None, ALU.add), "dt_u")
                own(dve, "dt_u")
                step(TS(dd, dtu, -1.0, None, ALU.add))
                up(TS(dz, dd, 0.0, None, ALU.is_equal), "dve_step")
                step(TS(dd, dd, 1e-30, None, ALU.max))
                step(V.reciprocal(dd, dd))
                step(TTo(dq, dte, dd, ALU.mult))
                need(dve, "dt_ln", l, 1)
                step(TTo(dq, dq, dln, ALU.mult))
                step(TTo(dz, dz, dte, ALU.mult))
                step(TTo(dq, dq, dz, ALU.add))
                up(TTo(dt_tok, dtm, dq, ALU.add), "dt_done")
                own(dve, "dt_done")
                need(dve, "a_exp", l, 1)
                up(STT(a_tok.rearrange("p (t h) -> p t h", t=TT), dt_tok.rearrange("p (t h) -> p t h", t=TT), -1.0,
                       rep(a_neg, TT), ALU.mult, ALU.mult), "dt_done")
                for j in range(4):
                    need(dve, "xbc_raw", l, j + 1)
                    for k in range(TAPS):
                        for c in (2 * j, 2 * j + 1):
                            w = col(l, "convw", c * TAPS + k)
                            if k == 0:
                                ins = TS(s_acc[:, c, :], s_raw[:, c, 0:T], w, None, ALU.mult)
                            else:
                                ins = STT(s_acc[:, c, :], s_raw[:, c, k:k + T], w, s_acc[:, c, :], ALU.mult, ALU.add)
                            up(ins, "conv" if k == TAPS - 1 else "dve_step")
                        own(dve, "conv" if k == TAPS - 1 else "dve_step")
                for c in range(XBC_TILES):
                    need(dve, "convsig", l, c + 1)
                    up(STT(s_xbc[:, c, :], s_acc[:, c, :], col(l, "convb", c), s_sig[:, c, :], ALU.add, ALU.mult), "xbcT")
                own(dve, "xbcT")
                b = bank(dve, ("cs", l))
                up(V.tensor_copy(cs, b[:, 0:24]), "cs_sb")
                own(dve, "cs_sb")

                def segment(q):
                    tt, g = q // 2, q % 2
                    b = bank(dve, ("seg", l, tt, g))
                    for h in range(4):
                        up(TS(s_L[:, q % 2, h, :], b[:, h * P:(h + 1) * P], cs[:, 8 * tt + 4 * g + h:8 * tt + 4 * g + h + 1],
                              0.0, ALU.subtract, ALU.min), "seg")

                def masked(tt):
                    b = bank(dve, ("cb", l, tt))
                    up(TTo(s_cb[:, tt], b[:, 0:256].rearrange("p (g n) -> p g n", g=2), rep(cst("mask4", 1, 128), 2),
                           ALU.mult), "cbm")
                    own(dve, "cbm")

                def weights(q):
                    tt, g = q // 2, q % 2
                    need(dve, "segexp", l, q + 1)
                    up(TTo(s_G[:, tt, 4 * g:4 * g + 4, :], s_L[:, q % 2], rep(s_cb[:, tt, g, :], 4), ALU.mult), "gmat")
                    own(dve, "gmat")

                for tt in range(TT):
                    segment(2 * tt)
                    segment(2 * tt + 1)
                    masked(tt)
                    weights(2 * tt)
                    weights(2 * tt + 1)
                for tt in range(TT):
                    need(dve, "zsig", l, tt + 1)
                    up(TTo(s_z[:, tt, :], s_z[:, tt, :], bank(dve, ("z", l, tt))[:, :], ALU.mult), "zsilu")
                own(dve, "zsilu")
                for tt in range(TT):
                    y = s_y[:, tt, :]
                    if tt:
                        b = bank(dve, ("yo", l))
                        up(TTo(s_sq.rearrange("p (h n) -> p h n", h=8), b[:, :].rearrange("p (h n) -> p h n", h=8),
                               over(ecs[:, 0:8], DH), ALU.mult), "yo_used")
                        own(dve, "yo_used")
                    need(dve, "dxs", l, tt + 1)
                    up(TTo(y, s_dx[:, tt, :], bank(dve, ("yd", l, tt))[:, :], ALU.add), "yd_used")
                    own(dve, "yd_used")
                    if tt:
                        step(TTo(y, y, s_sq, ALU.add))
                    step(TTo(y, y, s_z[:, tt, :], ALU.mult))
                    step(TTo(s_sq, y, y, ALU.mult))
                    up(V.tensor_reduce(g2[:, 0:2], s_sq.rearrange("p (g n) -> p g n", g=2), AX.X, ALU.add), "ssm_ss")
                    need(dve, "ssm_rstd", l, tt + 1)
                    up(TTo(y.rearrange("p (g n) -> p g n", g=2), y.rearrange("p (g n) -> p g n", g=2),
                           over(g2r[:, 0:2], 256), ALU.mult), "yssm")

            def retention(l):
                for j in range(4):
                    b = bank(dve, ("rot", l, j))
                    up(TTo(r_t, b[:, :].rearrange("p (c t) -> p c t", c=2), rep(cst("sin"), 2), ALU.mult), "rot_used")
                    own(dve, "rot_used")
                    need(dve, "qcos", l, j + 1)
                    up(TTo(r_qk[:, 2 * j:2 * j + 2, :], r_qk[:, 2 * j:2 * j + 2, :], r_t, ALU.add), "qkT")
                    own(dve, "qkT")
                for tt in range(TT):
                    need(dve, "rgsig", l, tt + 1)
                    up(TTo(r_g[:, tt, :], r_g[:, tt, :], bank(dve, ("rg", l, tt))[:, :], ALU.mult), "rgate")
                for tt in range(TT):
                    for q in range(2):
                        b = bank(dve, ("sc", l, tt, q))
                        up(TTo(r_sc[:, tt, q], b[:, :].rearrange("p (i n) -> p i n", i=4),
                               cst("decay", q, 512).rearrange("p (i n) -> p i n", i=4), ALU.mult), "scT")
                b = bank(dve, ("kt", l))
                up(TTo(r_kz.rearrange("p (h n) -> p h n", h=8), b[:, :].rearrange("p (h n) -> p h n", h=8),
                       over(cst("zeta"), DH), ALU.mult), "kz")
                for tt in range(TT):
                    y = r_y[:, tt, :]
                    yh = y.rearrange("p (h n) -> p h n", h=8)
                    if tt == 0:
                        up(V.tensor_copy(y, bank(dve, ("ry", l, 0))[:, :]), "ry_used")
                        own(dve, "ry_used")
                    else:
                        b = bank(dve, ("rc", l))
                        up(TTo(yh, b[:, :].rearrange("p (h n) -> p h n", h=8), over(cst("xi"), DH), ALU.mult), "rc_used")
                        own(dve, "rc_used")
                        up(TTo(y, y, bank(dve, ("ry", l, 1))[:, :], ALU.add), "ry_used")
                        own(dve, "ry_used")
                    step(TTo(r_sq, y, y, ALU.mult))
                    up(V.tensor_reduce(r8[:, 0:8], r_sq.rearrange("p (h n) -> p h n", h=8), AX.X, ALU.add), "ret_ss")
                    need(dve, "ret_rstd", l, tt + 1)
                    step(TTo(yh, yh, over(r8r[:, 0:8], DH), ALU.mult))
                    up(TTo(y, y, r_g[:, tt, :], ALU.mult), "yret")

            def rwkv(l):
                def c1024(ap):
                    return ap.rearrange("p c t -> p (c t)")

                def tile_pair(j):
                    c = RW_ORDER[j]
                    need(dve, "rw_raw", l, j + 1)
                    d = w_sq[:, 2 * (j % 2):2 * (j % 2) + 2, :]
                    step(TTo(d, w_raw[:, c:c + 2, 0:T], w_raw[:, c:c + 2, 1:1 + T], ALU.subtract))
                    for i in range(2):
                        up(STT(w_xm[:, c + i, :], d[:, i, :], col(l, "mu", c + i), w_raw[:, c + i, 1:1 + T],
                               ALU.mult, ALU.add), "xm")

                for j in range(5):
                    tile_pair(j)
                for tt in range(TT):
                    b = bank(dve, ("lw", l, tt))
                    up(TTo(w_lw[:, tt, :], b[:, :], row("w0"), ALU.add), "lwz")
                tile_pair(5)
                tile_pair(6)
                own(dve, "xm")
                kk, sq, k = w_kk, w_sq, w_xm[:, 4:8, :]
                step(TTo(kk, k, over(col(l, "kk", 0, 4), T), ALU.mult))
                up(TTo(sq, kk, kk, ALU.mult), "kksq")
                need(dve, "a_sig", l, 4)
                tmp = w_k
                step(STT(tmp, w_a, -1.0, over(col(l, "ka", 0, 4), T), ALU.add, ALU.mult))
                step(STT(c1024(k), c1024(tmp), 1.0, c1024(k), ALU.add, ALU.mult))
                for j in range(2):
                    b = bank(dve, ("kks", l, j))
                    up(TS(sq[:, 2 * j:2 * j + 2, :], b[:, :].rearrange("p (c t) -> p c t", c=2), 1e-24, None, ALU.max),
                       "kkmax")
                need(dve, "kkr", l, 1)
                step(V.reciprocal(c1024(sq), c1024(sq)))
                step(TTo(c1024(kk), c1024(kk), c1024(sq), ALU.mult))
                need(dve, "e2", l, 4)
                e1 = w_e1.rearrange("p c t s n -> p (c t) s n")
                ar = w_ar.rearrange("p c t s n -> p (c t) s n")
                ct = lambda ap: ap.rearrange("p c (t n) -> p (c t) n", t=TT)
                up(STT(ar[:, :, 0, :], ct(kk), -1.0, e1[:, :, 0, :], ALU.mult, ALU.mult), "ar")
                up(TTo(ar[:, :, 1, :], ct(w_xm[:, 0:4, :]), e1[:, :, 1, :], ALU.mult), "ar")
                step(TTo(c1024(w_b), c1024(kk), c1024(w_a), ALU.mult))
                up(TTo(c1024(w_k), c1024(k), c1024(w_e2), ALU.mult), "kb")
                up(TTo(c1024(w_b), c1024(w_b), c1024(w_e2), ALU.mult), "kb")
                step(TTo(c1024(sq), c1024(k), c1024(w_xm[:, 0:4, :]), ALU.mult))
                up(TTo(sq, sq, over(col(l, "rk", 0, 4), T), ALU.mult), "rk")
                up(V.reciprocal(rec4, w_e1[:, :, 1, 0, 0]), "dve_step")
                own(dve, "dve_step")
                up(TTo(sS, w_e1[:, :, 0, 1, P - 1], rec4, ALU.mult), "dve_step")
                v = w_xm[:, 8:12, :]
                if l == 0:
                    up(V.tensor_copy(vfirst, v), "v_fin")
                else:
                    need(dve, "vsig", 0, 4)
                    step(TTo(c1024(w_kk), c1024(vfirst), c1024(v), ALU.subtract))
                    step(TTo(c1024(w_kk), c1024(w_kk), c1024(w_a), ALU.mult))
                    up(TTo(c1024(v), c1024(v), c1024(w_kk), ALU.add), "v_fin")
                masks(l, 0)
                for v in range(LEVELS):
                    merge_blocks(l, 0, v)
                need(dve, "S_zero", l, 1)
                b = bank(dve, ("S", l))[:, :].rearrange("p (c n) -> p c n", c=CT)
                for q in range(2):
                    s = slice(64 * q, 64 * q + 64)
                    up(TTo(w_S[s, :, s], b[s, :, s], over(sS[s, :], DH), ALU.mult), "Sbd")
                masks(l, 1)
                for v in range(LEVELS):
                    merge_blocks(l, 1, v)
                    if v == 0:
                        centre(l, 0)
                    if v == 1:
                        group_norm(l, 0)
                centre(l, 1)
                group_norm(l, 1)

            def masks(l, tt):
                for g in range(2):
                    for h in range(4 * g, 4 * g + 4):
                        b = bank(dve, ("A", l, tt, h))
                        up(TTo(w_AT[:, h].rearrange("p q n -> p (q n)"), b[:, :], cst("mask4"), ALU.mult), "AT")
                    own(dve, "AT")
                    hs = slice(4 * g, 4 * g + 4)
                    step(TTo(w_XT[:, hs, :], w_AT[:, hs, 0, :], rep(cst("merge", 0, 128), 4), ALU.mult))
                    up(TTo(w_XT[:, hs, :], w_XT[:, hs, :], rep(cst("ident"), 4), ALU.add), "XTi")
                    if tt == 0 and g == 0:
                        b = bank(dve, ("bon", l))
                        up(V.tensor_copy(bons, b[:, 0:16]), "bon")
                        own(dve, "bon")
                    own(dve, "XTi")

            def merge_blocks(l, tt, v):
                for g in range(2):
                    hs = slice(4 * g, 4 * g + 4)
                    if v < LEVELS - 1:
                        b = bank(dve, ("XU", l, tt, v, g))
                        if v == 0:
                            need(dve, "Xi", l, 2 * tt + g + 1)
                        up(TTo(w_X[:, hs, :], w_X[:, hs, :], b[:, :].rearrange("p (h n) -> p h n", h=4), ALU.add), "Xu")
                    b = bank(dve, ("XTU", l, tt, v, g))
                    up(TTo(w_XT[:, hs, :], w_XT[:, hs, :], b[:, :].rearrange("p (h n) -> p h n", h=4), ALU.add), "XTu")
                own(dve, "XTu")
                if v < LEVELS - 1:
                    own(dve, "Xu")

            def h8(ap):
                return ap.rearrange("p (h n) -> p h n", h=8)

            def centre(l, tt):
                need(dve, "yraw", l, tt + 1)
                step(V.tensor_reduce(m8[:, 0:8], h8(w_y), AX.X, ALU.add))
                step(TS(m8[:, 0:8], m8[:, 0:8], 1.0 / DH, None, ALU.mult))
                step(TTo(h8(w_y), h8(w_y), over(m8[:, 0:8], DH), ALU.subtract))
                step(TTo(w_t, w_y, w_y, ALU.mult))
                up(V.tensor_reduce(v8[:, 0:8], h8(w_t), AX.X, ALU.add), "rw_ss")
                own(dve, "rw_ss")

            def group_norm(l, tt):
                step(TTo(h8(w_t), h8(w_vt[:, tt, :]), over(bons[:, 8 * tt:8 * tt + 8], DH), ALU.mult))
                need(dve, "rw_rstd", l, tt + 1)
                step(TTo(h8(w_y), h8(w_y), over(v8r[:, 0:8], DH), ALU.mult))
                step(TTo(w_y, w_y, row("gnw"), ALU.mult))
                step(TTo(w_y, w_y, row("gnb"), ALU.add))
                step(TTo(w_y, w_y, w_t, ALU.add))
                up(TTo(w_o[:, tt, :], w_y, w_g[:, tt, :], ALU.mult), "yrw")

            def merge(l):
                n = 0
                for i in range(3):
                    for half in range(2):
                        for tt in range(TT):
                            need(dve, "gsig", l, n + 1)
                            b = bank(dve, ("br", l, i, half, tt))
                            out = xn[:, tt, half * W:(half + 1) * W]
                            if n >= 4:
                                dve.wait_ge(sem("merged"), l * 12 + n - 1)
                            up(TTo(prod[:, n % 2, :], b[:, :], gates[:, n, :], ALU.mult), "brprod")
                            own(dve, "brprod")
                            if i:
                                ins = TTo(out, out, prod[:, n % 2, :], ALU.add)
                            else:
                                ins = V.tensor_copy(out, prod[:, n % 2, :])
                            up(ins, "merged")
                            n += 1
                for j in range(4):
                    b = bank(dve, ("mT", l, j))
                    up(V.tensor_copy(hT[:, 2 * j:2 * j + 2, :], b[:, :].rearrange("p (c t) -> p c t", c=2)), "mT")
                for tt in range(TT):
                    for half in range(2):
                        b = bank(dve, ("out", l, half, tt))
                        x = X[:, tt, half * W:(half + 1) * W]
                        up(TTo(x, x, b[:, :], ALU.add), "xmix")

            def split_low():
                for j in range(4):
                    need(dve, "hTh", 0, j + 1)
                    s = slice(2 * j, 2 * j + 2)
                    up(TTo(hTl[:, s, :], hT[:, s, :], plain(hTh[:, s, :]), ALU.subtract), "hTl")

            def dense():
                tasks = {}
                for ch in range(DENSE_CH):
                    g, u = last(DENSE_SEQ, "g", ch), last(DENSE_SEQ, "u", ch)
                    end = len(DENSE_SEQ) - 1
                    tasks.setdefault(min(g + LAG, end), []).append(("gated", ch, g))
                    tasks.setdefault(min(u + LAG, end), []).append(("hidden", ch, u))
                    tasks.setdefault(min(u + LAG + 2, end), []).append(("low", ch, u))
                n_slab = DENSE_SLAB0 - 1
                for n, (kind, ch, q) in enumerate(DENSE_SEQ):
                    n_slab += q == 0
                    need(dve, "q_hi", 0, n + 1)
                    hi, lo = ring(n)
                    up(TTo(lo, slab[:, n_slab % SLOTS, q * QUARTER:(q + 1) * QUARTER], plain(hi), ALU.subtract), "q_lo")
                    for what, c, at_q in tasks.get(n, []):
                        for j in range(2 if c < DENSE_CH - 1 else 1):
                            s = f_s[:, j, :]
                            if what == "gated":
                                need(dve, "fsig", 0, 2 * c + j + 1)
                                up(TTo(s, s, psum[j][:, :], ALU.mult), "fgt")
                            elif what == "hidden":
                                need(dve, "q_used", 0, at_q + 1)
                                need(dve, "fgt", 0, 2 * c + j + 1)
                                up(TTo(s, s, psum[2 + j][:, :], ALU.mult), "fhid")
                            else:
                                need(dve, "fhh", 0, 2 * c + j + 1)
                                hs = slice(2 * j, 2 * j + 2)
                                up(TTo(f_hl[:, c % 2, hs, :].rearrange("p f t -> p (f t)"), s,
                                       plain(f_hh[:, c % 2, hs, :]).rearrange("p f t -> p (f t)"), ALU.subtract), "fhl")
                need(dve, "q_used", 0, len(DENSE_SEQ))
                for tt in range(TT):
                    for half in range(2):
                        x = X[:, tt, half * W:(half + 1) * W]
                        up(TTo(x, x, psum[4 + 2 * tt + half][:, :], ALU.add), "xffn")
                own(dve, "xffn")

            def route():
                for a in (gate9, sel9, pos9):
                    up(V.memset(a[:, :, N_EXP:], 0.0), "dve_step")
                up(V.tensor_copy(lg, bank(dve, ("route",))[:, 0:16]), "lg")
                own(dve, "lg")
                for tt in range(TT):
                    s = slice(8 * tt, 8 * tt + 8)
                    step(V.max(mx8[:, s], lg[:, s]))
                    step(V.max_index(idx8[:, s], mx8[:, s], lg[:, s]))
                    step(V.tensor_copy(idxf[:, s], idx8[:, s]))
                    step(TS(oh1[:, s], cst("iota8"), idxf[:, 8 * tt:8 * tt + 1], None, ALU.is_equal))
                    step(TS(oh2[:, s], cst("iota8"), idxf[:, 8 * tt + 1:8 * tt + 2], None, ALU.is_equal))
                    up(TTo(sel9[:, tt, 0:N_EXP], oh1[:, s], oh2[:, s], ALU.add), "sel")
                    up(TTo(ex[:, tt:tt + 1], mx8[:, 8 * tt + 1:8 * tt + 2], mx8[:, 8 * tt:8 * tt + 1], ALU.subtract), "top")
                    dve.wait_ge(sem("topexp"), tt + 1)
                    w1, w2 = w12[:, 2 * tt:2 * tt + 1], w12[:, 2 * tt + 1:2 * tt + 2]
                    step(TS(w1, ex[:, tt:tt + 1], 1.0, None, ALU.add))
                    step(V.reciprocal(w1, w1))
                    step(TTo(w2, w1, ex[:, tt:tt + 1], ALU.mult))
                    step(TS(oh1[:, s], oh1[:, s], w1, None, ALU.mult))
                    up(STT(gate9[:, tt, 0:N_EXP], oh2[:, s], w2, oh1[:, s], ALU.mult, ALU.add), "sel")
                b = bank(dve, ("rank",))
                up(V.tensor_copy(pos9[:, :, 0:N_EXP], b[:, 0:16].rearrange("p (t e) -> p t e", t=TT)), "rank")
                up(V.tensor_reduce(flagf[:, 0:1], b[:, 16:24], AX.X, ALU.max), "rank")
                own(dve, "rank")
                up(V.tensor_copy(flag[:, :], flagf[:, 0:1]), "e_flag")

            def experts(p):
                def onehot(g, e0, par):
                    for i, src in enumerate((pos9, sel9, gate9)):
                        up(V.tensor_copy(cur[:, 2 * i:2 * i + 2], src[:, :, bass.ds(e0, 1)]
                                         .rearrange("p t e -> p (t e)")), "m_cur")
                    dve.wait_ge(sem("m_cur"), 3 * g + 3)
                    for i, dst in ((1, e_P), (2, e_G)):
                        for tt in range(TT):
                            up(TS(dst[:, tt, :], cst("slot"), cur[:, tt:tt + 1], cur[:, 2 * i + tt:2 * i + tt + 1],
                                  ALU.is_equal, ALU.mult), "m_onehot")

                def scaled(g):
                    for j in range(2):
                        dve.wait_ge(sem("m_gather"), 3 * g + j + 1)
                        up(TTo(e_xf[:, 4 * j:4 * j + 4, :], psum[6 + j][:, :].rearrange("p (k n) -> p k n", k=4),
                               over(col(DEPTH - 1, "norm2", 4 * j, 4), P), ALU.mult), "m_xf")

                def xlow(g, par):
                    for j in range(2):
                        dve.wait_ge(sem("m_xh"), 2 * g + j + 1)
                        s = slice(4 * j, 4 * j + 4)
                        up(TTo(e_xl[:, par, s, :], e_xf[:, s, :], plain(e_xh[:, par, s, :]), ALU.subtract), "m_xl")

                def add(e, tt):
                    for half in range(2):
                        dve.wait_ge(sem("m_comb"), 4 * p + 4 * e + 2 * tt + half + 1)
                        x = X[:, tt, half * W:(half + 1) * W]
                        up(TTo(x, x, psum[6 + half][:, :], ALU.add), "m_add")

                def task(what, a, e, e0, par):
                    if what == "gated":
                        s = e_s[:, a % 2, :]
                        dve.wait_ge(sem("m_sig"), 7 * e + a + 1)
                        up(TTo(s, s, psum[2 * (a % 2)][:, :], ALU.mult), "m_gated")
                    elif what == "hidden":
                        dve.wait_ge(sem("m_gated"), 7 * e + a + 1)
                        dve.wait_ge(sem("m_used"), RING + NQ * e + last(MOE_SEQ, "u", a) + 1)
                        up(TTo(e_h[:, a % 2, :], e_s[:, a % 2, :], psum[2 * (a % 2) + 1][:, :], ALU.mult), "m_hid")
                    elif what == "low":
                        dve.wait_ge(sem("m_hh"), 7 * e + a + 1)
                        up(TTo(e_hl[:, a % 2], psum[6 + a % 2][:, :].rearrange("p (f n) -> p f n", f=4),
                               plain(e_hh[:, a % 2]), ALU.subtract), "m_hl")
                    elif what == "add":
                        add(e, a)
                    elif what == "onehot":
                        onehot(e + p + 1, e0 + 1, 1 - par)
                    elif what == "scaled":
                        scaled(e + p + 1)
                    else:
                        xlow(e + p + 1, 1 - par)

                if p:
                    step(TS(pos9, pos9, -float(P), None, ALU.add))
                up(V.memset(e_GT[:, 1, :], 0.0), "m_zero")
                up(V.memset(psum[4][:, :], 0.0), "dve_step")
                up(V.memset(psum[5][:, :], 0.0), "m_zero")
                onehot(9 * p, 0, 0)
                scaled(9 * p)
                xlow(9 * p, 0)
                plan = moe_plan()[2]
                with dve.Fori(0, N_EXP // 2) as pair:
                    for par in range(2):
                        e = 2 * pair + (par + N_EXP * p)
                        for i in range(NQ):
                            h = i // 2
                            hi, lo = ring(i)
                            dve.wait_ge(sem("m_hi"), NQ * e + i + 1)
                            up(TTo(lo, e_raw[h % RAW][:, (i % 2) * QUARTER:(i % 2 + 1) * QUARTER], plain(hi),
                                   ALU.subtract), "m_lo")
                            for what, a in plan[i]:
                                task(what, a, e, 2 * pair + par, par)
                for tt in range(TT):
                    add(N_EXP * (p + 1), tt)
                own_adds = 4 * (p + 1) + 4 * N_EXP * (p + 1)
                dve.wait_ge(sem("m_add"), own_adds)

            dve.wait_ge(sem("pcol"), 16)
            x_ready(dve, 0, 1)
            for l in range(DEPTH):
                norm(l, 2 * l, "norm1")
                dve.wait_ge(sem("const"), 16)
                ssm(l)
                retention(l)
                rwkv(l)
                merge(l)
                norm(l, 2 * l + 1, "norm2")
                if l == 0:
                    split_low()
                    dense()
                else:
                    route()
            experts(0)
            overflow(dve, experts)
            up(V.tensor_copy(cur[:, 0:1], cur[:, 1:2]), "x_final")
            dve.wait_ge(sem("rstd_final"), 1)
            dve.wait_ge(sem("finw"), 16)
            for tt in range(TT):
                up(STT(xn[:, tt, :], X[:, tt, :], rs[:, tt:tt + 1], finw, ALU.mult, ALU.mult), "normed")

        @block.gpsimd
        def _(pool):
            G = nc.gpsimd

            def step(ins):
                up(ins, "pool_step")
                own(pool, "pool_step")

            def rsqrt(out, x, n, scale, eps, sig):
                step(G.tensor_scalar(out, x, scale, eps, ALU.mult, ALU.add))
                up(G.tensor_tensor(out, out, cst("neghalf").to_broadcast([P, n]), ALU.pow), sig)

            def norm(n):
                for tt in range(TT):
                    need(pool, "sumsq", n, tt + 1)
                    rsqrt(rs[:, tt:tt + 1], ss[:, tt:tt + 1], 1, 1.0 / D, RMS_EPS, "rstd")

            def ssm(l):
                if l:
                    need(pool, "xffn", 0, 4)
                up(G.memset(s_raw[:, :, 0:3], 0.0), "xbc_zero")
                need(pool, "dt_done", l, 2)
                up(G.tensor_copy(s_ab, over(a_tok, P)), "a_bcast")
                h8 = lambda ap: ap.rearrange("p (h n) -> p h n", h=8)
                for tt in range(TT):
                    need(pool, "xs_tok", l, tt + 1)
                    up(G.tensor_tensor(h8(s_xdt[:, tt, :]), h8(s_xs[:, tt, :]), over(dt_tok[:, 8 * tt:8 * tt + 8], DH),
                                       ALU.mult), "xdt")
                need(pool, "cs_exp", l, 1)
                own(pool, "xdt")
                up(G.tensor_tensor(h8(s_xdd), h8(s_xdt[:, 0, :]), over(ecs[:, 8:16], DH), ALU.mult), "xdd")
                for tt in range(TT):
                    up(G.tensor_tensor(h8(s_dx[:, tt, :]), h8(s_xs[:, tt, :]), over(row("dskip"), DH), ALU.mult), "dxs")
                for tt in range(TT):
                    need(pool, "ssm_ss", l, tt + 1)
                    rsqrt(g2r[:, 0:2], g2[:, 0:2], 2, 1.0 / 256, RMS_EPS, "ssm_rstd")

            def retention(l):
                need(pool, "yT", l, 8)
                up(G.memset(r_kv, 0.0), "kv_zero")
                for j in range(4):
                    need(pool, "qraw", l, j + 1)
                    s = slice(2 * j, 2 * j + 2)
                    up(G.tensor_tensor(r_qk[:, s, :], r_raw[:, s, :], rep(cst("cos"), 2), ALU.mult), "qcos")
                for tt in range(TT):
                    need(pool, "ret_ss", l, tt + 1)
                    rsqrt(r8r[:, 0:8], r8[:, 0:8], 8, 1.0 / DH, RMS_EPS, "ret_rstd")

            def rwkv(l):
                need(pool, "yT", l, 10)
                up(G.memset(w_raw[:, :, 0:1], 0.0), "raw_zero")
                up(G.memset(w_S, 0.0), "S_zero")
                for tt in range(TT):
                    for v in range(LEVELS):
                        for g in range(2):
                            if v == 0:
                                need(pool, "AT", l, 8 * tt + 4 * g + 4)
                            else:
                                bank(pool, ("P1", l, tt, v - 1, g))
                            hs = slice(4 * g, 4 * g + 4)
                            up(G.tensor_tensor(w_LT[:, hs, :], w_AT[:, hs, 0, :], rep(cst("merge", v + 1, 128), 4),
                                               ALU.mult), "LTm")
                        if tt == 1 and v == 1:
                            group_rsqrt(l, 0)
                group_rsqrt(l, 1)

            def group_rsqrt(l, tt):
                need(pool, "rw_ss", l, tt + 1)
                rsqrt(v8r[:, 0:8], v8[:, 0:8], 8, 1.0 / DH, GN_EPS, "rw_rstd")

            pool.wait_ge(sem("const_first"), 16)
            for l in range(DEPTH):
                norm(2 * l)
                pool.wait_ge(sem("const"), 16)
                ssm(l)
                retention(l)
                rwkv(l)
                norm(2 * l + 1)
            pool.wait_ge(sem("sumsq"), 2 * (2 * DEPTH + 1))
            rsqrt(rs, ss, 2, 1.0 / D, RMS_EPS, "rstd_final")


def kernel(**inputs):
    import concourse.bacc as bacc
    from concourse.bass_utils import run_bass_kernel_spmd

    a = {k: np.ascontiguousarray(v) for k, v in inputs.items()}

    def tiles(v):
        v = np.asarray(v)
        return v.reshape(v.shape[0], -1, P).transpose(0, 2, 1)

    v0 = np.concatenate([np.zeros((DEPTH - len(a["rw_v0"]), W), np.float32), a["rw_v0"]], 0)
    cw = a["ssm_conv_w"].reshape(DEPTH, XBC_TILES, P, TAPS).transpose(0, 2, 1, 3).reshape(DEPTH, P, -1)
    pcol = np.concatenate([tiles(a["norm1_w"]), tiles(a["norm2_w"]), tiles(a["rw_mu"]), tiles(a["rw_k_k"]),
                           tiles(a["rw_k_a"]), tiles(a["rw_a0"]), tiles(a["rw_r_k"].reshape(DEPTH, -1)), tiles(v0),
                           tiles(a["ssm_norm_w"]), cw, tiles(a["ssm_conv_b"])], 2)
    prow = np.concatenate([a["rw_w0"], a["rw_gn_w"], a["rw_gn_b"], a["ssm_dt_bias"], a["ssm_a_log"], a["ssm_d"]], 1)
    feeds = dict(x=a["x"], const=constants(), pcol=np.ascontiguousarray(pcol), prow=np.ascontiguousarray(prow))
    for name in ("w_in", "rw_w_up", "rw_a_up", "rw_g_up", "rw_v_down", "rw_v_up", "w_branch", "w_out", "ffn_wg",
                 "ffn_wu", "ffn_wd", "moe_router", "moe_wg", "moe_wu", "moe_wd", "final_norm_w"):
        feeds[name] = a[name]
    nc = bacc.Bacc("TRN2", target_bir_lowering=False, num_devices=1)
    t = {k: nc.dram_tensor(f"in_{k}", v.shape, F32, kind="ExternalInput").ap() for k, v in feeds.items()}
    t["out"] = nc.dram_tensor("out", a["x"].shape, F32, kind="ExternalOutput").ap()
    trunk(nc, t)
    r = run_bass_kernel_spmd(nc, [{f"in_{k}": v for k, v in feeds.items()}], core_ids=[0])
    return r.results[0]["out"]
```
